# Optimizing a Trainium2 kernel written in Bass

```python
import math
import jax, jax.numpy as jnp
from jax import lax
import numpy as np

D_MODEL = 1024
BATCH = 1
SEQ = 512
DEPTH = 2

N_MIXERS = 2
HEAD_DIM = 64
N_HEADS = D_MODEL // HEAD_DIM
RWKV_DECAY_LORA = 64
RWKV_AAA_LORA = 64
RWKV_GATE_LORA = 128
RWKV_GN_EPS = 64e-5
MOBA_BLOCK = 256
MOBA_TOPK = 3
Q_CHUNK = 128
ROPE_THETA = 10000.0
MEM_TOKENS = 256
MEM_HEADS = 4
MEM_HEAD_DIM = D_MODEL // MEM_HEADS
MOE_GROUPS = 4
MOE_EXPERTS_PER_GROUP = 8
MOE_EXPERTS = MOE_GROUPS * MOE_EXPERTS_PER_GROUP
MOE_TOPK = 2
MOE_FF = D_MODEL // 2
MOE_ROW_BLOCK = 128
RMS_EPS = 1e-6
NEG_INF = -1e30
N_RWKV_LAYERS = (DEPTH + N_MIXERS - 1) // N_MIXERS
N_MOBA_LAYERS = DEPTH // N_MIXERS

kernel_name = "hybrid_rwkv7_moba_memxattn_hmoe"

F32 = jnp.float32

def rms_norm(x, g):
    xf = x.astype(F32)
    y = xf * lax.rsqrt(jnp.mean(xf * xf, axis=-1, keepdims=True) + RMS_EPS)
    return (y * g.astype(F32)).astype(x.dtype)

def rotary(t, positions):
    half = t.shape[-1] // 2
    inv = ROPE_THETA ** (-jnp.arange(half, dtype=F32) * 2.0 / t.shape[-1])
    ang = positions.astype(F32)[..., None] * inv
    cos = jnp.cos(ang)[:, :, None, :]
    sin = jnp.sin(ang)[:, :, None, :]
    tf = t.astype(F32)
    t1, t2 = tf[..., :half], tf[..., half:]
    return jnp.concatenate([t1 * cos - t2 * sin, t2 * cos + t1 * sin], axis=-1).astype(t.dtype)

def rwkv7_time_mix(h, mu, w0, w1, w2, a0, a1, a2, g1, g2, k_k, k_a, r_k, w_rkv, lnx_g, lnx_b, w_o):
    B, T, C = h.shape
    dx = jnp.pad(h, ((0, 0), (1, 0), (0, 0)))[:, :T] - h
    xr, xw, xk, xv, xa, xg = [h + dx * mu[s] for s in range(6)]
    r = xr @ w_rkv[0]
    k = xk @ w_rkv[1]
    v = xv @ w_rkv[2]
    w = -jax.nn.softplus(-(w0 + jnp.tanh(xw @ w1) @ w2)) - 0.5
    a = jax.nn.sigmoid(a0 + (xa @ a1) @ a2)
    g = jax.nn.sigmoid(xg @ g1) @ g2

    def heads(t):
        return t.reshape(B, T, N_HEADS, HEAD_DIM).astype(F32)

    kk = heads(k * k_k)
    kk = kk / jnp.maximum(jnp.sqrt(jnp.sum(kk * kk, axis=-1, keepdims=True)), 1e-12)
    k = k * (1.0 + (a - 1.0) * k_a)
    r_h, k_h, v_h, a_h = heads(r), heads(k), heads(v), heads(a)
    decay = jnp.exp(-jnp.exp(heads(w)))

    def step(S, inp):
        r_t, d_t, k_t, v_t, kk_t, akk_t = inp
        s_kk = jnp.einsum('bhvk,bhk->bhv', S, kk_t)
        S = S * d_t[:, :, None, :] - s_kk[..., None] * akk_t[:, :, None, :] + v_t[..., None] * k_t[:, :, None, :]
        return S, jnp.einsum('bhvk,bhk->bhv', S, r_t)

    def tm(t):
        return jnp.swapaxes(t, 0, 1)

    S0 = jnp.zeros((B, N_HEADS, HEAD_DIM, HEAD_DIM), F32)
    _, o = lax.scan(step, S0, (tm(r_h), tm(decay), tm(k_h), tm(v_h), tm(kk), tm(kk * a_h)))
    o = tm(o)
    mean = jnp.mean(o, axis=-1, keepdims=True)
    var = jnp.mean((o - mean) ** 2, axis=-1, keepdims=True)
    o = ((o - mean) * lax.rsqrt(var + RWKV_GN_EPS)).reshape(B, T, C) * lnx_g.astype(F32) + lnx_b.astype(F32)
    bonus = (jnp.sum(r_h * k_h * r_k.astype(F32), axis=-1, keepdims=True) * v_h).reshape(B, T, C)
    return ((o + bonus).astype(h.dtype) * g) @ w_o

def moba_attention(h, positions, w_qkv, w_o):
    B, T, C = h.shape
    qkv = (h @ w_qkv).reshape(B, T, 3, N_HEADS, HEAD_DIM)
    q = jnp.transpose(rotary(qkv[:, :, 0], positions), (0, 2, 1, 3))
    k = jnp.transpose(rotary(qkv[:, :, 1], positions), (0, 2, 1, 3))
    v = jnp.transpose(qkv[:, :, 2], (0, 2, 1, 3))
    n_blk = -(-T // MOBA_BLOCK)
    pad = n_blk * MOBA_BLOCK - T
    kb = jnp.pad(k, ((0, 0), (0, 0), (0, pad), (0, 0))).reshape(B, N_HEADS, n_blk, MOBA_BLOCK, HEAD_DIM)
    vb = jnp.pad(v, ((0, 0), (0, 0), (0, pad), (0, 0))).reshape(B, N_HEADS, n_blk, MOBA_BLOCK, HEAD_DIM)
    scale = 1.0 / math.sqrt(HEAD_DIM)
    topk_eff = min(MOBA_TOPK, n_blk - 1)
    q_blk = jnp.arange(T) // MOBA_BLOCK
    if topk_eff > 0:
        kmean = jnp.mean(kb.astype(F32), axis=3)
        gate = jnp.einsum('bhtd,bhnd->bhtn', q.astype(F32), kmean)
        past = jnp.arange(n_blk)[None, :] < q_blk[:, None]
        gate = jnp.where(past, gate, NEG_INF)
        _, sel = lax.top_k(gate, topk_eff)
        sel_valid = jnp.arange(topk_eff)[None, :] < q_blk[:, None]
    n_qc = T // Q_CHUNK
    h_ar = jnp.arange(N_HEADS)[:, None, None]
    q_off = jnp.arange(Q_CHUNK)
    k_off = jnp.arange(MOBA_BLOCK)

    def chunk(i):
        b = i // n_qc
        q0 = (i % n_qc) * Q_CHUNK
        qc = lax.dynamic_slice_in_dim(q[b], q0, Q_CHUNK, axis=1)
        kb_b = kb[b]
        vb_b = vb[b]
        own = q0 // MOBA_BLOCK
        k_own = lax.dynamic_index_in_dim(kb_b, own, axis=1, keepdims=False)
        v_own = lax.dynamic_index_in_dim(vb_b, own, axis=1, keepdims=False)
        s_own = jnp.einsum('hqd,hkd->hqk', qc, k_own, preferred_element_type=F32) * scale
        causal = (own * MOBA_BLOCK + k_off)[None, :] <= (q0 + q_off)[:, None]
        s_own = jnp.where(causal[None], s_own, NEG_INF)
        if topk_eff > 0:
            sel_c = lax.dynamic_slice_in_dim(sel[b], q0, Q_CHUNK, axis=1)
            valid_c = lax.dynamic_slice_in_dim(sel_valid, q0, Q_CHUNK, axis=0)
            k_sel = kb_b[h_ar, sel_c]
            v_sel = vb_b[h_ar, sel_c]
            s_sel = jnp.einsum('hqd,hqnkd->hqnk', qc, k_sel, preferred_element_type=F32) * scale
            s_sel = jnp.where(valid_c[None, :, :, None], s_sel, NEG_INF)
            s_sel = s_sel.reshape(N_HEADS, Q_CHUNK, topk_eff * MOBA_BLOCK)
            p = jax.nn.softmax(jnp.concatenate([s_sel, s_own], axis=-1), axis=-1)
            p_sel = p[..., :topk_eff * MOBA_BLOCK].reshape(N_HEADS, Q_CHUNK, topk_eff, MOBA_BLOCK).astype(v.dtype)
            p_own = p[..., topk_eff * MOBA_BLOCK:].astype(v.dtype)
            return (jnp.einsum('hqnk,hqnkd->hqd', p_sel, v_sel)
                    + jnp.einsum('hqk,hkd->hqd', p_own, v_own))
        p_own = jax.nn.softmax(s_own, axis=-1).astype(v.dtype)
        return jnp.einsum('hqk,hkd->hqd', p_own, v_own)

    outs = lax.map(chunk, jnp.arange(B * n_qc))
    o = outs.reshape(B, n_qc, N_HEADS, Q_CHUNK, HEAD_DIM).transpose(0, 1, 3, 2, 4).reshape(B, T, C)
    return o @ w_o

def mem_cross_attention(h, mem_n, w_q, w_kv, w_o):
    B, T, C = h.shape
    M = mem_n.shape[1]
    q = (h @ w_q).reshape(B, T, MEM_HEADS, MEM_HEAD_DIM)
    kv = (mem_n @ w_kv).reshape(B, M, 2, MEM_HEADS, MEM_HEAD_DIM)
    s = jnp.einsum('bthd,bmhd->bhtm', q, kv[:, :, 0], preferred_element_type=F32) / math.sqrt(MEM_HEAD_DIM)
    p = jax.nn.softmax(s, axis=-1).astype(h.dtype)
    o = jnp.einsum('bhtm,bmhd->bthd', p, kv[:, :, 1]).reshape(B, T, C)
    return o @ w_o

def hierarchical_moe(h, w_grp, b_grp, w_exp, b_exp, w1, w3, w2):
    N, C = h.shape
    R = MOE_ROW_BLOCK
    g_logits = jnp.einsum('nc,cg->ng', h, w_grp, preferred_element_type=F32) + b_grp.astype(F32)
    p_g, g_idx = lax.top_k(jax.nn.softmax(g_logits, axis=-1), 1)
    e_logits = (jnp.einsum('nc,ce->ne', h, w_exp, preferred_element_type=F32) + b_exp.astype(F32))
    e_logits = e_logits.reshape(N, MOE_GROUPS, MOE_EXPERTS_PER_GROUP)
    e_logits = jnp.take_along_axis(e_logits, g_idx[:, :, None], axis=1)[:, 0]
    p_e, e_loc = lax.top_k(jax.nn.softmax(e_logits, axis=-1), MOE_TOPK)
    gate = p_g * p_e / jnp.sum(p_e, axis=-1, keepdims=True)
    expert = g_idx * MOE_EXPERTS_PER_GROUP + e_loc

    P = N * MOE_TOPK
    flat_e = expert.reshape(-1)
    flat_tok = jnp.repeat(jnp.arange(N, dtype=jnp.int32), MOE_TOPK)
    flat_gate = gate.reshape(-1)
    order = jnp.argsort(flat_e)
    e_sorted = flat_e[order]
    counts = jnp.bincount(flat_e, length=MOE_EXPERTS)
    padded = (counts + R - 1) // R * R
    start = jnp.cumsum(counts) - counts
    pad_end = jnp.cumsum(padded)
    pad_start = pad_end - padded
    dest = pad_start[e_sorted] + (jnp.arange(P) - start[e_sorted])
    n_blocks = (P + MOE_EXPERTS * (R - 1) + R - 1) // R
    n_rows = n_blocks * R
    row_tok = jnp.zeros((n_rows,), jnp.int32).at[dest].set(flat_tok[order])
    row_gate = jnp.zeros((n_rows,), F32).at[dest].set(flat_gate[order])
    block_expert = jnp.minimum(jnp.searchsorted(pad_end, jnp.arange(n_blocks) * R, side='right'),
                               MOE_EXPERTS - 1)
    x_rows = h[row_tok].reshape(n_blocks, R, C)

    def expert_block(args):
        xb, e = args
        return (jax.nn.silu(xb @ w1[e]) * (xb @ w3[e])) @ w2[e]

    y = lax.map(expert_block, (x_rows, block_expert)).reshape(n_rows, C)
    out = jnp.zeros((N, C), F32).at[row_tok].add(y.astype(F32) * row_gate[:, None])
    return out.astype(h.dtype)

def setup_inputs(seed: int = 0) -> dict:
    key = jax.random.key(seed)
    ks = iter(jax.random.split(key, 40))
    D = D_MODEL

    def nrm(shape, scale):
        return jax.random.normal(next(ks), shape, F32) * scale

    def gain(shape):
        return 1.0 + nrm(shape, 0.05)

    NR, NM = N_RWKV_LAYERS, N_MOBA_LAYERS
    return {
        "x": nrm((BATCH, SEQ, D), 1.0),
        "mem": nrm((BATCH, MEM_TOKENS, D), 1.0),
        "positions": jnp.tile(jnp.arange(SEQ, dtype=jnp.int32)[None, :], (BATCH, 1)),
        "ln_mix": gain((DEPTH, D)),
        "ln_mem": gain((DEPTH, D)),
        "ln_memkv": gain((DEPTH, D)),
        "ln_ffn": gain((DEPTH, D)),
        "rw_mu": jax.random.uniform(next(ks), (NR, 6, D), F32),
        "rw_w0": nrm((NR, D), 0.5),
        "rw_w1": nrm((NR, D, RWKV_DECAY_LORA), D ** -0.5),
        "rw_w2": nrm((NR, RWKV_DECAY_LORA, D), 0.1 * RWKV_DECAY_LORA ** -0.5),
        "rw_a0": nrm((NR, D), 0.3),
        "rw_a1": nrm((NR, D, RWKV_AAA_LORA), D ** -0.5),
        "rw_a2": nrm((NR, RWKV_AAA_LORA, D), 0.1 * RWKV_AAA_LORA ** -0.5),
        "rw_g1": nrm((NR, D, RWKV_GATE_LORA), D ** -0.5),
        "rw_g2": nrm((NR, RWKV_GATE_LORA, D), RWKV_GATE_LORA ** -0.5),
        "rw_kk": 0.85 + nrm((NR, D), 0.05),
        "rw_ka": 1.0 + nrm((NR, D), 0.05),
        "rw_rk": nrm((NR, N_HEADS, HEAD_DIM), 0.3),
        "rw_wrkv": nrm((NR, 3, D, D), D ** -0.5),
        "rw_lnx_g": gain((NR, D)),
        "rw_lnx_b": nrm((NR, D), 0.01),
        "rw_wo": nrm((NR, D, D), D ** -0.5),
        "mb_wqkv": nrm((NM, D, 3 * D), D ** -0.5),
        "mb_wo": nrm((NM, D, D), D ** -0.5),
        "mx_wq": nrm((DEPTH, D, D), D ** -0.5),
        "mx_wkv": nrm((DEPTH, D, 2 * D), D ** -0.5),
        "mx_wo": nrm((DEPTH, D, D), D ** -0.5),
        "moe_wg": nrm((DEPTH, D, MOE_GROUPS), D ** -0.5),
        "moe_bg": nrm((DEPTH, MOE_GROUPS), 0.01),
        "moe_we": nrm((DEPTH, D, MOE_EXPERTS), D ** -0.5),
        "moe_be": nrm((DEPTH, MOE_EXPERTS), 0.01),
        "moe_w1": nrm((DEPTH, MOE_EXPERTS, D, MOE_FF), D ** -0.5),
        "moe_w3": nrm((DEPTH, MOE_EXPERTS, D, MOE_FF), D ** -0.5),
        "moe_w2": nrm((DEPTH, MOE_EXPERTS, MOE_FF, D), MOE_FF ** -0.5),
        "ln_f": gain((D,)),
    }

def reference(x, mem, positions, ln_mix, ln_mem, ln_memkv, ln_ffn,
              rw_mu, rw_w0, rw_w1, rw_w2, rw_a0, rw_a1, rw_a2, rw_g1, rw_g2, rw_kk, rw_ka, rw_rk,
              rw_wrkv, rw_lnx_g, rw_lnx_b, rw_wo,
              mb_wqkv, mb_wo,
              mx_wq, mx_wkv, mx_wo,
              moe_wg, moe_bg, moe_we, moe_be, moe_w1, moe_w3, moe_w2,
              ln_f):
    B, T, C = x.shape
    for i in range(DEPTH):
        j = i // N_MIXERS
        h = rms_norm(x, ln_mix[i])
        if i % N_MIXERS == 0:
            mixed = rwkv7_time_mix(h, rw_mu[j], rw_w0[j], rw_w1[j], rw_w2[j], rw_a0[j], rw_a1[j], rw_a2[j],
                                   rw_g1[j], rw_g2[j], rw_kk[j], rw_ka[j], rw_rk[j], rw_wrkv[j],
                                   rw_lnx_g[j], rw_lnx_b[j], rw_wo[j])
        else:
            mixed = moba_attention(h, positions, mb_wqkv[j], mb_wo[j])
        x = x + mixed
        x = x + mem_cross_attention(rms_norm(x, ln_mem[i]), rms_norm(mem, ln_memkv[i]),
                                    mx_wq[i], mx_wkv[i], mx_wo[i])
        h2 = rms_norm(x, ln_ffn[i]).reshape(B * T, C)
        x = x + hierarchical_moe(h2, moe_wg[i], moe_bg[i], moe_we[i], moe_be[i],
                                 moe_w1[i], moe_w3[i], moe_w2[i]).reshape(B, T, C)
    return rms_norm(x, ln_f)


_drawn_inputs = setup_inputs


def setup_inputs(seed=0):
    import zlib

    import numpy as np

    out = dict(_drawn_inputs(seed))
    spreads = {}
    factors = {'ln_mem': 2.837, 'rw_w1': 3.755, 'rw_lnx_b': 2.853, 'moe_bg': 2.751, 'moe_be': 2.787}
    for name, (base, spread) in spreads.items():
        noise = np.random.default_rng([zlib.crc32(name.encode()), seed]).standard_normal(out[name].shape)
        drawn = base * np.exp(spread * noise) if base else spread * noise
        out[name] = __import__('jax').numpy.asarray(drawn.astype(out[name].dtype))
    for name, factor in factors.items():
        out[name] = (out[name] * factor).astype(out[name].dtype)
    return out
```

```python
import math

import concourse.bass as bass
import numpy as np
from concourse import mybir
from contextlib import ExitStack

F32 = mybir.dt.float32
I32 = mybir.dt.int32
ALU = mybir.AluOpType
ACT = mybir.ActivationFunctionType
AX = mybir.AxisListType.X

P = 128
T, C, M = 512, 1024, 256
KT, TT, MT = C // P, T // P, M // P
L = 64
CH = T // L
PAIRS = KT
NH = C // L
HB = 512
XH, XD = 4, 256
G, EG, E, FF = 4, 8, 32, 512
FT = FF // P
BR = 64
NB = 2 * T // BR + E - 1
PRE = 2
NBP = NB + 1
RMS_EPS, GN_EPS, NEG = 1e-6, 64e-5, -1e30
DECAY = math.exp(-0.5)
TWO_PI_PARTS = (6.28125, 0.0019350051879882812, 3.019916e-07)
ROUND_MAGIC = 1.5 * 2.0 ** 23
PI_BELOW = 3.1415925

LN = ["ln_mix0", "ln_mix1", "ln_mem0", "ln_mem1", "ln_kv0", "ln_kv1", "ln_ffn0", "ln_ffn1"]
RW = ["mu0", "mu1", "mu2", "mu3", "mu4", "mu5", "w0", "a0", "kk", "ka", "rk"]
COL = {n: i * KT for i, n in enumerate(LN + RW)}


def bank_group_order():
    o = [("params",)]
    norm = lambda n: [("norm", n, k) for k in range(KT)]
    both = lambda s: [(s, half, t) for half in range(2) for t in range(TT)]
    per = lambda s, *a: [(s, *a, k) for k in range(KT)]
    o += norm(0) + [("hidden_wa",), ("hidden_g",)] + per("decay") + per("rate") + both("gate")
    o += per("r") + per("k") + both("v") + [("knorm",), ("knorm_t",)] + per("kscale") + [("bonus",)]
    o += [("gn_t", p, half) for p in range(PAIRS) for half in range(2)] + both("rwkv_out")
    n = 1
    for l in range(2):
        if l == 1:
            o += norm(n) + both("mq") + both("mk") + both("mv") + per("mqT") + per("mkT")
            n += 1
            o += [("ms", 0, q) for q in range(TT)]
            for h in range(NH):
                if h + 1 < NH:
                    o += [("ms", h + 1, q) for q in range(TT)]
                o += [("mp", h, q) for q in range(TT)] + [("mo", h)]
            o += per("moT") + both("moba_out")
        o += [("memT", l, i) for i in range(KT // 2)] + per("xk", l)
        o += [("xv", l, half, m) for half in range(2) for m in range(MT)] + norm(n) + per("xq", l)
        n += 1
        o += [("xs", l, 0, i) for i in range(2)]
        for h in range(XH):
            if h + 1 < XH:
                o += [("xs", l, h + 1, i) for i in range(2)]
            o += [("xp", l, h, m) for m in range(MT)] + [("xo", l, h, c) for c in range(2)]
        o += [("xattn_out", l, half, t) for half in range(2) for t in range(TT)]
        o += norm(n) + [("route", l), ("rank", l)]
        n += 1
    return o


def chunk_steps():
    pe = ["gram_b", "gram_k", "betaT", "kappaT", "y0"]
    for i in range(6):
        pe += ([f"x{i + 1}"] if i < 4 else []) + ([f"y{i + 1}"] if i < 5 else []) + ([f"t{i + 1}"] if i else [])
    pe += ["rhs", "u", "o", "s"]
    act = ["decay", "growth", "alpha0", "alpha1", "rho0", "rho1", "beta", "kappa", "y0"]
    act += [f"x{i + 1}" for i in range(4)] + ["y5", "rhs", "u", "o"]
    dve = ["a_rest", "a_first", "rho", "beta0", "beta1", "kappa0", "kappa1", "x0", "t0", "bn", "n", "k"]
    dve += ["y1", "y2", "y3", "y4"]
    dve.insert(dve.index("y2") + 1, "t2")
    dve.insert(dve.index("y3") + 1, "t3")
    dve.insert(dve.index("y4") + 1, "t4")
    dve += ["t5", "t6", "s_add", "s"]
    return pe, act, dve


def trunk(nc, x_in, mem, positions, ln_mix, ln_mem, ln_memkv, ln_ffn, rw_mu, rw_w0, rw_w1, rw_w2, rw_a0, rw_a1,
          rw_a2, rw_g1, rw_g2, rw_kk, rw_ka, rw_rk, rw_wrkv, rw_lnx_g, rw_lnx_b, rw_wo, mb_wqkv, mb_wo, mx_wq,
          mx_wkv, mx_wo, moe_wg, moe_bg, moe_we, moe_be, moe_w1, moe_w3, moe_w2, ln_f, out, stop=99):
    ctx = ExitStack()
    with ctx:
        def sb(name, shape, dt=F32):
            return ctx.enter_context(nc.sbuf_tensor(name, shape, dt))

        def sem(name):
            return ctx.enter_context(nc.semaphore(name))

        ORDER = bank_group_order()
        WHERE = {name: i for i, name in enumerate(ORDER)}

        big = sb("big", [P, 12 * C * 4])

        def region(i, n=1):
            return big[:, i * 4096:(i + n) * 4096]

        def tiles(r, a):
            return r.rearrange("p (a b) -> p a b", a=a)

        x = tiles(region(0), TT)
        XN = tiles(region(1), TT)
        HT = tiles(region(3), KT)
        W = [tiles(region(4 + i), KT) for i in range(2)]
        R = [region(6 + i) for i in range(6)]
        RE = region(2)
        keep = tiles(R[5], KT)[:, KT - 1]

        ident = sb("ident", [P, P])
        ones = sb("ones", [P, P])
        before = sb("before", [P, P])
        m_strict = sb("m_strict", [P, 2, L])
        m_incl = sb("m_incl", [P, 2, L])
        m_minus = sb("m_minus", [P, 2, 2, L])
        m_causal = sb("m_causal", [P, P])
        pair_sel = sb("pair_sel", [P, 2])
        head_sel = sb("head_sel", [NH, PAIRS, P])
        par = sb("par", [P, (len(LN) + len(RW)) * KT])
        half_w0a0 = sb("half_w0a0", [P, 2 * KT])
        one_minus_ka = sb("one_minus_ka", [P, KT])
        bonus = sb("bonus", [P, PAIRS, CH])
        scratch = sb("scratch", [P, 1024])
        hid_wa, hid_g = scratch[:, 0:T], scratch[:, T:2 * T]
        cosn, sinn = (scratch[:, i * P:(i + 1) * P].rearrange("p (t j) -> p t j", t=TT) for i in range(2))
        ang = [scratch[:, (2 + i) * P:(3 + i) * P] for i in range(4)]
        zero = sb("zero", [P, 256])
        ss = sb("ss", [P, TT])
        rstd = sb("rstd", [P, TT])
        mss = sb("mss", [P, MT])
        mrstd = sb("mrstd", [P, MT])
        nmax = sb("nmax", [P, 2, 8])
        esum = sb("esum", [P, 2, 8])
        einv = sb("einv", [P, 2, 8])
        posi = sb("posi", [P, TT], I32)
        posf = sb("posf", [P, TT])
        inv_freq = sb("inv_freq", [P, 32])
        dest_i = sb("dest_i", [P, 2, TT], I32)
        gate2 = sb("gate2", [P, 2, TT])
        tok_i = sb("tok_i", [P, TT], I32)
        idx = [sb(f"idx{i}", [BR, 1], I32) for i in range(2)]
        item_i = sb("item_i", [1, NBP + 1], I32)
        item_no = sb("item_no", [1, NBP])
        iota = sb("iota", [P, E])[:]
        krt = sb("krt", [P, TT * NH])
        krT = hid_wa[0:NH, :]
        gst = sb("gst", [P, PAIRS * CH])
        e2 = sb("e2", [P, TT * (G + 1)])

        ps = [ctx.enter_context(nc.psum_tensor(f"ps{i}", [P, HB], F32)) for i in range(8)]

        slot_tok = [nc.dram_tensor(f"slot_tok{l}", (NBP * BR, 1), I32, kind="Internal").ap() for l in range(2)]
        h_rows = [nc.dram_tensor(f"h_rows{l}", (T, C), F32, kind="Internal").ap() for l in range(2)]
        y_rows = [nc.dram_tensor(f"y_rows{l}", (NBP * BR, C), F32, kind="Internal").ap() for l in range(2)]

        lw1 = RE[:, 0:512].rearrange("p (k n) -> p k n", k=KT)
        la1 = RE[:, 512:1024].rearrange("p (k n) -> p k n", k=KT)
        lg1 = RE[:, 1024:2048].rearrange("p (k n) -> p k n", k=KT)
        lwa2 = RE[:, 2048:3072]
        lg2 = RE[:, 3072:4096]
        prow, qrow = W[0][:, 0, 0:P], W[0][:, 1, 0:P]

        filled = sem("filled")
        emptied = [sem(f"emptied{b}") for b in range(8)]
        x_loaded, params_loaded, lora_loaded = sem("x_loaded"), sem("params_loaded"), sem("lora_loaded")
        w_loaded = [sem(f"w_loaded{i}") for i in range(2)]
        consts = sem("consts")
        dve_chain, act_chain, pool_chain = sem("dve_chain"), sem("act_chain"), sem("pool_chain")
        squares_done, var_ready, std_ready, xn_ready = (sem(n) for n in
                                                        ("squares_done", "var_ready", "std_ready", "xn_ready"))
        mixed = sem("mixed")
        tanh_g, hid_g_ready, kk_sq, kvar_ready, kstd_ready, krinv_ready, prod_ready, pre_done = (
            sem(n) for n in ("tanh_g", "hid_g_ready", "kk_sq", "kvar_ready", "kstd_ready", "krinv_ready",
                             "prod_ready", "pre_done"))
        scans_done, act_rwkv = sem("scans_done"), sem("act_rwkv")
        pe_done = [sem(f"pe_done{g}") for g in range(2)]
        act_done = [sem(f"act_done{g}") for g in range(2)]
        dve_done = [sem(f"dve_done{g}") for g in range(2)]
        centred, gn_sq, gvar_ready, gstd_ready, gn_done, lnx_loaded = (
            sem(n) for n in ("centred", "gn_sq", "gvar_ready", "gstd_ready", "gn_done", "lnx_loaded"))
        mem_loaded, mem_sq, mvar_ready, mstd_ready, memn_ready = (
            sem(n) for n in ("mem_loaded", "mem_sq", "mvar_ready", "mstd_ready", "memn_ready"))
        xmax_ready, xexp_done, xprob_ready = sem("xmax_ready"), sem("xexp_done"), sem("xprob_ready")
        pos_loaded, angles_ready, sines_ready = sem("pos_loaded"), sem("angles_ready"), sem("sines_ready")
        rot_products, rotated = sem("rot_products"), sem("rotated")
        mmax_ready, mexp_done, msum_inv = sem("mmax_ready"), sem("mexp_done"), sem("msum_inv")
        router_loaded, ids_zeroed, rows_stored, ids_stored = (
            sem(n) for n in ("router_loaded", "ids_zeroed", "rows_stored", "ids_stored"))
        picks_ready, dest_ready, items_ready = sem("picks_ready"), sem("dest_ready"), sem("items_ready")
        e_w = [[sem(f"expert_w{l}{i}") for i in range(6)] for l in range(2)]
        ids_loaded = [[sem(f"ids_loaded{l}{b}") for b in range(2)] for l in range(2)]
        gathered = [[sem(f"gathered{l}{b}") for b in range(2)] for l in range(2)]
        y_stored = [[sem(f"y_stored{l}{b}") for b in range(2)] for l in range(2)]
        rowsT, rowsT_out, up_done, th_done, act_ready, down_done, y_act, y_dve, a_part = (
            [sem(f"{n}{l}") for l in range(2)] for n in
            ("rowsT", "rowsT_out", "up_done", "th_done", "act_ready", "down_done", "y_act", "y_dve", "a_part"))
        combined_loaded = [[sem(f"combined_loaded{l}{s}") for s in range(8)] for l in range(2)]
        x_updated = sem("x_updated")
        y_zeroed = sem("y_zeroed")
        all_stored = sem("all_stored")
        counts_in, gates_exp = sem("counts_in"), sem("gates_exp")
        lnf_loaded, out_ready, out_stored = sem("lnf_loaded"), sem("out_ready"), sem("out_stored")
        NORM_MEM, NORM_FFN = [1, 4], [2, 5]

        def wait_filled(eng, name):
            eng.wait_ge(filled, WHERE[name] + 1)

        def wait_emptied(eng, name):
            g = WHERE[name]
            eng.wait_ge(emptied[g % 8], g // 8 + 1)

        def bank(name):
            return ps[WHERE[name] % 8]

        def empties(ins, name):
            ins.then_inc(emptied[WHERE[name] % 8], 1)

        def col(name, k):
            return par[:, COL[name] + k:COL[name] + k + 1]

        GP = PAIRS // 2

        groups = []
        for g in range(2):
            views, end = {}, 0
            for name, size in ([("ar", 2 * GP * L)]
                               + [(m, GP * P) for m in ("alpha", "rho", "beta", "kappa", "X", "Y", "Tm", "N", "K",
                                                        "Bn", "bt", "kt")]
                               + [(m, GP * L) for m in ("rhs", "u", "dec", "gro", "S")]):
                r = region(1 if g == 0 else 4, 2)[:, end:end + size]
                end += size
                if name == "ar":
                    views[name] = r.rearrange("p (q s t) -> p q s t", q=GP, s=2)
                elif size == GP * P:
                    views[name] = r.rearrange("p (q h t) -> p q h t", q=GP, h=2)
                else:
                    views[name] = r.rearrange("p (q t) -> p q t", q=GP)
            groups.append(views)
        r_all, k_all, v_all = R[1], R[0], R[2]
        lam_all, ak_all, g_all, kk_all = R[3], R[4], R[5], region(3)
        by_chunk = lambda r: r.rearrange("p (q c t) -> p q c t", q=PAIRS, c=CH)
        PE_S, ACT_S, DVE_S = chunk_steps()


        def after(done, steps, step, c):
            return c * len(steps) + (steps.index(step) + 2)

        def wait_pe(eng, g, c, step):
            eng.wait_ge(pe_done[g], after(pe_done, PE_S, step, c))

        def wait_act(eng, g, c, step):
            eng.wait_ge(act_done[g], after(act_done, ACT_S, step, c))

        def wait_dve(eng, g, c, step):
            eng.wait_ge(dve_done[g], after(dve_done, DVE_S, step, c))

        def chunk_of(r, g, c):
            return by_chunk(r)[:, g * GP:(g + 1) * GP, bass.ds(c, 1), :].rearrange("p q o t -> p q (o t)")

        qxT = tiles(R[0], KT)
        kxT = R[1][:, 0:2048].rearrange("p (k m) -> p k m", k=KT)
        vx = R[1][:, 2048:4096].rearrange("p (m n) -> p m n", m=MT)
        memT = R[2][:, 0:2048].rearrange("p (k m) -> p k m", k=KT)
        memn = R[2][:, 2048:4096].rearrange("p (m n) -> p m n", m=MT)
        oxT = tiles(R[3], KT)
        px = R[4][:, 0:2048].rearrange("p (b q m) -> p b q m", b=2, q=TT)
        pxT = R[5][:, 0:2048].rearrange("p (b m q) -> p b m q", b=2, m=MT)

        qm, km, vm = (tiles(R[i], TT) for i in range(3))
        qmT, kmT = tiles(R[3], KT), tiles(R[4], KT)
        pm = R[5].rearrange("p (b q k) -> p b q k", b=2, q=TT)
        pmT = RE.rearrange("p (b q k) -> p b q k", b=2, q=TT)
        rot = RE.rearrange("p (b s n) -> p b s n", b=4, s=2)

        ew = [[R[3 * b + i] for i in range(3)] for b in range(2)]
        hg = [RE[0:BR, b * 1024:(b + 1) * 1024] for b in range(2)]
        hgT = [region(3)[:, b * 512:(b + 1) * 512].rearrange("p (k j) -> p k j", k=KT) for b in range(2)]
        th = [region(3)[:, 1024 + b * 256:1280 + b * 256].rearrange("p (f j) -> p f j", f=FT) for b in range(2)]
        ga = [region(3)[:, 1536 + b * 256:1792 + b * 256].rearrange("p (f j) -> p f j", f=FT) for b in range(2)]
        hact = [region(3)[:, 2048 + b * 256:2304 + b * 256].rearrange("p (f j) -> p f j", f=FT) for b in range(2)]
        y = [RE[0:BR, 2048 + b * 1024:3072 + b * 1024] for b in range(2)]
        wr = RE[:, 0:KT * 36].rearrange("p (k n) -> p k n", k=KT)
        br = RE[:, 288:324]
        at = [KT * 36 + 36]

        def tmp(*shape):
            size = int(np.prod(shape))
            r = RE[:, at[0]:at[0] + size]
            at[0] += size
            names = "abc"[:len(shape)]
            if len(shape) == 1:
                return r
            return r.rearrange(f"p ({' '.join(names)}) -> p {' '.join(names)}", **dict(zip(names, shape)))

        logits, gmax, gidx, g1h, gsum = tmp(TT, 36), tmp(TT), tmp(TT), tmp(TT, G), tmp(TT)
        t4_, sel, prod = tmp(TT, G), tmp(TT, EG), tmp(TT, EG, G)
        m1, i1, m2, i2, t8 = tmp(TT), tmp(TT), tmp(TT), tmp(TT), tmp(TT, EG)
        o1, o2, cnt, rank, dst2 = tmp(TT, E), tmp(TT, E), tmp(TT, E), tmp(TT, E), tmp(2, TT)
        nblk, cum, one32, t32, step8 = tmp(E), tmp(E), tmp(E), tmp(E, 8), tmp(8)
        itemc, itf = tmp(NBP, E), tmp(NBP + 1)
        assert at[0] <= 4096
        combined = [R[i // 4][:, (i % 4) * C:(i % 4 + 1) * C] for i in range(8)]

        loads = []

        def halves(w, last):
            for half in range(2):
                loads.append((w[:, half * HB:(half + 1) * HB].rearrange("(k p) n -> p k n", p=P), last(half)))

        chan_last = lambda s, *a: (lambda half: (s, *a, 4 * half + 3))
        tok_last = lambda s, *a: (lambda half: (s, *a, half, TT - 1))
        halves(rw_wrkv[0, 0], chan_last("r"))
        halves(rw_wrkv[0, 1], chan_last("k"))
        halves(rw_wrkv[0, 2], tok_last("v"))
        halves(rw_wo[0], tok_last("rwkv_out"))
        for l in range(2):
            if l == 1:
                for i, s in enumerate(("mq", "mk", "mv")):
                    halves(mb_wqkv[0, :, i * C:(i + 1) * C], tok_last(s))
                halves(mb_wo[0], tok_last("moba_out"))
            halves(mx_wkv[l, :, 0:C], chan_last("xk", l))
            halves(mx_wkv[l, :, C:2 * C], lambda half, l=l: ("xv", l, half, MT - 1))
            halves(mx_wq[l], chan_last("xq", l))
            halves(mx_wo[l], tok_last("xattn_out", l))
        USE = {}
        for j, (_, last) in enumerate(loads):
            USE.setdefault(last[:-1] if last[0] in ("r", "k", "xk", "xq") else last[:-1], []).append(j)

        def load_index(stage, half):
            if stage[0] in ("r", "k", "xk", "xq"):
                return USE[stage][half]
            return USE[stage + (half,)][0]

        def unstacks(eng, copy, p, half):
            name = ("gn_t", p, half)
            wait_filled(eng, name)
            src = bank(name)[0:L, :].rearrange("p (c h t) -> p c h t", c=4, h=2)
            for hh in range(2):
                dst = HT[hh * L:(hh + 1) * L, p, half * 256:(half + 1) * 256].rearrange("p (c t) -> p c t", c=4)
                ins = copy(dst, src[:, :, hh, :])
            empties(ins, name)

        block = ctx.enter_context(nc.Block())

        @block.sync
        def _(sp):
            sp.dma_start(x, x_in[0].rearrange("(t p) c -> p t c", p=P)).then_inc(x_loaded, 16)
            sp.dma_start(lw1, rw_w1[0].rearrange("(k p) n -> p k n", p=P)).then_inc(lora_loaded, 16)
            sp.dma_start(la1, rw_a1[0].rearrange("(k p) n -> p k n", p=P)).then_inc(lora_loaded, 16)
            sp.dma_start(lg1, rw_g1[0].rearrange("(k p) n -> p k n", p=P)).then_inc(lora_loaded, 16)
            sp.dma_start(lwa2[0:64, :], rw_w2[0]).then_inc(lora_loaded, 16)
            sp.dma_start(lwa2[64:128, :], rw_a2[0]).then_inc(lora_loaded, 16)
            sp.dma_start(lg2, rw_g2[0]).then_inc(lora_loaded, 16)
            sp.dma_start(posi[:], positions[0].rearrange("(t p) -> p t", p=P), allow_slow_non_contiguous=True).then_inc(pos_loaded, 16)
            wait_emptied(sp, ("params",))

            def load(j):
                if j >= 2:
                    wait_filled(sp, loads[j - 2][1])
                sp.dma_start(W[j % 2], loads[j][0]).then_inc(w_loaded[j % 2], 16)

            def load_mem(l):
                sp.dma_start(memn, mem[0].rearrange("(m p) c -> p m c", p=P)).then_inc(mem_loaded, 16)

            def experts(l):
                sp.wait_ge(items_ready, l + 1)
                count = sp.value_load(item_i[0:1, NBP:NBP + 1], min_val=0, max_val=NB)

                def up_matrices(b, e, past):
                    sp.wait_ge(up_done[l], past + 1 + PRE)
                    for s, w in ((0, moe_w1), (1, moe_w3)):
                        dst = ew[b][s].rearrange("p (k n) -> p k n", k=KT)
                        src = w[l].rearrange("e (k p) n -> e p k n", p=P)[bass.ds(e, 1)]
                        sp.dma_start(dst, src.rearrange("o p k n -> (o p) k n")).then_inc(e_w[l][3 * b + s], 16)

                first = sp.value_load(item_i[0:1, 0:1], min_val=0, max_val=E - 1)
                up_matrices(0, first, -1)
                with sp.Fori(0, NBP // 2) as i:
                    for b in range(2):
                        with sp.If(count > i * 2 + b + 1):
                            e = sp.value_load(item_i[0:1, bass.ds(i * 2 + b + 1, 1)], min_val=0, max_val=E - 1)
                            up_matrices(1 - b, e, i * 2 + b - 1)
                        with sp.If(count > i * 2 + b):
                            e = sp.value_load(item_i[0:1, bass.ds(i * 2 + b, 1)], min_val=0, max_val=E - 1)
                            sp.wait_ge(down_done[l], i * 2 + b - 1 + PRE)
                            dst = ew[b][2].rearrange("p (k n) -> p k n", k=FT)
                            src = moe_w2[l].rearrange("e (k p) n -> e p k n", p=P)[bass.ds(e, 1)]
                            sp.dma_start(dst, src.rearrange("o p k n -> (o p) k n")).then_inc(e_w[l][3 * b + 2], 16)

            for j in range(6):
                load(j)
            sp.wait_ge(consts, 1)
            for l in range(2):
                sp.dma_start(y_rows[l][2 * T:].rearrange("(p a) (s c) -> p (a s) c", p=P, s=C // 256),
                             zero[:].unsqueeze(1).to_broadcast([P, (NBP * BR - 2 * T) // P * (C // 256), 256])
                             ).then_inc(y_zeroed, 16)
            for g in range(2):
                sp.wait_ge(pe_done[g], 1 + CH * len(PE_S))
                sp.wait_ge(act_done[g], 1 + CH * len(ACT_S))
                sp.wait_ge(dve_done[g], 1 + CH * len(DVE_S))
            load(6)
            load(7)
            for i, v in enumerate((rw_lnx_g, rw_lnx_b)):
                for hh in range(2):
                    sp.dma_start(RE[hh * 64:hh * 64 + 64, i * 512:(i + 1) * 512].rearrange("p (q v) -> p q v", q=PAIRS),
                                 v[0].rearrange("(q h v) -> h q v", q=PAIRS, h=2)[hh].partition_broadcast(64)
                                 ).then_inc(lnx_loaded, 16)
            sp.wait_ge(gn_done, 1)
            load_mem(0)
            j = 8
            for l in range(2):
                if l == 1:
                    for _ in range(4):
                        load(j)
                        j += 1
                    load(j)
                    load(j + 1)
                    j += 2
                    wait_emptied(sp, ("moT", KT - 1))
                    load_mem(1)
                for _ in range(8):
                    load(j)
                    j += 1
                if l == 1:
                    wait_emptied(sp, ("mo", NH - 1))
                else:
                    sp.wait_ge(gn_done, 1)
                sp.dma_start(wr[:, :, 0:G], moe_wg[l].rearrange("(k p) n -> p k n", p=P)).then_inc(router_loaded, 16)
                sp.dma_start(wr[:, :, G:G + E], moe_we[l].rearrange("(k p) n -> p k n", p=P)).then_inc(router_loaded, 16)
                sp.dma_start(br[:, 0:G], moe_bg[l].partition_broadcast(P)).then_inc(router_loaded, 16)
                sp.dma_start(br[:, G:G + E], moe_be[l].partition_broadcast(P)).then_inc(router_loaded, 16)
                sp.wait_ge(xn_ready, 4 * NORM_FFN[l] + 4)
                sp.dma_start(h_rows[l].rearrange("(t p) c -> p t c", p=P), XN).then_inc(rows_stored, 16)
                if l == 0:
                    load(j)
                    load(j + 1)
                    j += 2
                experts(l)
            sp.wait_ge(x_updated, 16)
            sp.dma_start(R[2][:, 0:C], ln_f.partition_broadcast(P)).then_inc(lnf_loaded, 16)
            for t in range(TT):
                sp.wait_ge(out_ready, t + 1)
                sp.dma_start(out[0, t * P:(t + 1) * P, :], XN[:, t]).then_inc(out_stored, 16)
            sp.wait_ge(out_stored, 16 * TT)

        @block.gpsimd
        def _(pool):
            n = [0]

            def link(ins):
                n[0] += 1
                ins.then_inc(pool_chain, 1)
                pool.wait_ge(pool_chain, n[0])

            def triangle(out, in_, op, fill, base=0, mult=1, pattern=None):
                return pool.affine_select(out=out, in_=in_, compare_op=op, fill=fill, base=base,
                                          pattern=pattern or [[-1, P]], channel_multiplier=mult)

            link(pool.memset(ident[:], 0.0))
            link(pool.memset(zero[:], 0.0))
            triangle(ident[:], ident[:], ALU.not_equal, 1.0).then_inc(consts, 1)
            link(pool.memset(ones[:], 1.0))
            link(triangle(before[:], ones[:], ALU.is_gt, 0.0, mult=-1, pattern=[[1, P]]))
            flat = lambda m: m[:].rearrange("p h t -> p (h t)")
            link(triangle(flat(m_strict), ones[:], ALU.is_gt, 0.0, mult=-1, pattern=[[1, P]]))
            link(triangle(flat(m_incl), ones[:], ALU.is_ge, 0.0, mult=-1, pattern=[[1, P]]))
            link(pool.memset(m_strict[0:64, 1, :], 0.0))
            link(pool.memset(m_incl[0:64, 1, :], 0.0))
            link(pool.tensor_scalar(m_minus[:, 0], m_strict[:], -1.0, None, ALU.mult))
            link(pool.tensor_scalar(m_minus[:, 1], m_incl[:], -1.0, None, ALU.mult))
            link(pool.memset(m_causal[:], 0.0))
            link(triangle(m_causal[:], m_causal[:], ALU.is_ge, NEG))
            link(pool.memset(pair_sel[:], 0.0))
            link(pool.memset(pair_sel[0:64, 0:1], 1.0))
            link(pool.memset(pair_sel[64:128, 1:2], 1.0))
            link(pool.memset(keep, 1.0))
            link(pool.memset(keep.rearrange("p (c t) -> p c t", t=L)[:, :, 0:1], 0.0))
            link(pool.memset(head_sel[:], 0.0))
            hs = head_sel[:].rearrange("h q (s j) -> h q s j", s=2)
            link(pool.affine_select(out=hs, in_=hs, compare_op=ALU.not_equal, fill=1.0, base=0,
                                    pattern=[[-2, PAIRS], [-1, 2], [0, L]], channel_multiplier=1))
            for j in range(32):
                pool.memset(inv_freq[:, j:j + 1], float(np.float32(10000.0) ** np.float32(-j * 2.0 / 64)))
            link(pool.iota(tok_i[:], [[P, TT]], base=0, channel_multiplier=1))
            link(pool.iota(iota, [[1, E]], base=0, channel_multiplier=0, allow_small_or_imprecise_dtypes=True))
            pool.iota(item_no[:], [[1, NBP]], base=0, channel_multiplier=0, allow_small_or_imprecise_dtypes=True
                      ).then_inc(consts, 1)
            zeros = region(6)[0:NBP, 0:BR].bitcast(I32)
            link(pool.memset(zeros, 0))
            for l in range(2):
                pool.dma_start(slot_tok[l].rearrange("(a b) o -> a (b o)", b=BR), zeros).then_inc(ids_zeroed, 16)
            pool.wait_ge(ids_zeroed, 32)

            for l in range(2):
                for k in range(2):
                    for t in range(TT):
                        if k == 0 and t == 0:
                            pool.wait_ge(dest_ready, l + 1)
                        pool.indirect_dma_start(
                            slot_tok[l], bass.IndirectOffsetOnAxis(ap=dest_i[:, k, t:t + 1], axis=0),
                            tok_i[:, t:t + 1], None).then_inc(ids_stored, 16)
                pool.wait_ge(ids_stored, 16 * 8 * (l + 1))
                pool.wait_ge(rows_stored, 16 * (l + 1))
                pool.wait_ge(items_ready, l + 1)
                count = pool.value_load(item_i[0:1, NBP:NBP + 1], min_val=0, max_val=NB)
                ids_of = slot_tok[l].rearrange("(a b) o -> a b o", b=BR)
                for n_block in range(NBP):
                    b = n_block % 2
                    with pool.If(count + 1 > n_block):
                        pool.wait_ge(rowsT[l], n_block - 1 + PRE)
                        pool.dma_start(idx[b][:], ids_of[n_block]).then_inc(ids_loaded[l][b], 16)
                        pool.wait_ge(ids_loaded[l][b], 16 * (n_block // 2 + 1))
                        pool.indirect_dma_start(hg[b], None, h_rows[l],
                                                bass.IndirectOffsetOnAxis(ap=idx[b][:], axis=0)
                                                ).then_inc(gathered[l][b], 16)
                pool.wait_ge(all_stored, l + 1)
                for s in range(8):
                    t, k = s // 2, s % 2
                    pool.indirect_dma_start(combined[s], None, y_rows[l],
                                            bass.IndirectOffsetOnAxis(ap=dest_i[:, k, t:t + 1], axis=0)
                                            ).then_inc(combined_loaded[l][s], 16)

        @block.scalar
        def _(act):
            A = nc.scalar.activation
            n = [0]

            def link(ins):
                n[0] += 1
                ins.then_inc(act_chain, 1)
                act.wait_ge(act_chain, n[0])

            def wait_x(norm, t):
                if norm == 0:
                    act.wait_ge(x_loaded, 16)
                elif norm == 1:
                    wait_emptied(act, ("rwkv_out", 1, t))
                elif norm in (2, 5):
                    wait_emptied(act, ("xattn_out", norm // 3, 1, t))
                elif norm == 3:
                    act.wait_ge(x_updated, 2 * t + 2)
                elif norm == 4:
                    wait_emptied(act, ("moba_out", 1, t))
                else:
                    act.wait_ge(x_updated, 8 + 2 * t + 2)

            def norm_squares(norm):
                for t in range(TT):
                    wait_x(norm, t)
                    A(XN[:, t], x[:, t], ACT.Square, accum_out=ss[:, t:t + 1]).then_inc(squares_done, 1)
                act.wait_ge(var_ready, norm + 1)
                A(rstd[:], ss[:], ACT.Sqrt).then_inc(std_ready, 1)

            def norm_out(norm, gain):
                for k in range(0, KT, 2):
                    name = ("norm", norm, k)
                    wait_filled(act, name)
                    empties(A(HT[:, k], bank(name)[:], ACT.Copy, scale=col(gain, k)), name)

            for i, v in enumerate((ln_mix, ln_mem, ln_memkv, ln_ffn)):
                act.dma_start(prow[16 * i:16 * i + 16, :], v.rearrange("l (k p) -> (l k) p", p=P)
                              ).then_inc(params_loaded, 16)
            act.dma_start(qrow[0:48, :], rw_mu[0].rearrange("s (k p) -> (s k) p", p=P)).then_inc(params_loaded, 16)
            for i, v in enumerate((rw_w0, rw_a0, rw_kk, rw_ka)):
                act.dma_start(qrow[48 + 8 * i:56 + 8 * i, :], v[0].rearrange("(k p) -> k p", p=P)
                              ).then_inc(params_loaded, 16)
            act.dma_start(qrow[80:88, :], rw_rk[0].rearrange("(k h) d -> k (h d)", h=2)).then_inc(params_loaded, 16)

            norm_squares(0)
            norm_out(0, "ln_mix0")
            wait_filled(act, ("hidden_wa",))
            A(hid_wa[0:64, :], bank(("hidden_wa",))[0:64, :], ACT.Tanh)
            empties(A(hid_wa[64:128, :], bank(("hidden_wa",))[64:128, :], ACT.Copy), ("hidden_wa",))
            wait_filled(act, ("hidden_g",))
            empties(A(hid_g, bank(("hidden_g",))[:], ACT.Tanh, scale=0.5), ("hidden_g",))
            for stage, dst, c in (("decay", lam_all, 0), ("rate", ak_all, KT)):
                for p in range(KT):
                    wait_filled(act, (stage, p))
                    empties(A(tiles(dst, KT)[:, p], bank((stage, p))[:], ACT.Tanh, scale=0.5,
                              bias=half_w0a0[:, c + p:c + p + 1]), (stage, p))

            def stack(dst, name, half, t):
                wait_filled(act, name)
                src = bank(name)[:].rearrange("p (q h v) -> p q h v", q=4, h=2)
                d = by_chunk(dst)
                for even in range(2):
                    for hh in range(2):
                        last = A(d[hh * 64:hh * 64 + 64, 4 * half:4 * half + 4, 2 * t + even, :],
                                 src[even * 64:even * 64 + 64, :, hh, :], ACT.Copy)
                empties(last, name)

            act.wait_ge(scans_done, KT)
            for half in range(2):
                for t in range(TT):
                    stack(g_all, ("gate", half, t), half, t)
            for stage, dst in (("r", r_all), ("k", k_all)):
                for p in range(KT):
                    wait_filled(act, (stage, p))
                    empties(A(tiles(dst, KT)[:, p], bank((stage, p))[:], ACT.Copy), (stage, p))
            for p in range(KT):
                wait_emptied(act, ("k", p))
                if p == 0:
                    act.wait_ge(mixed, 6 * KT)
                A(tiles(region(1), KT)[:, p], tiles(k_all, KT)[:, p], ACT.Square, scale=col("kk", p)
                  ).then_inc(kk_sq, 1)
            for half in range(2):
                for t in range(TT):
                    stack(v_all, ("v", half, t), half, t)
            act.wait_ge(kvar_ready, 1)
            A(krt[:], krt[:], ACT.Sqrt).then_inc(kstd_ready, 1)

            for g in range(2):
                act.wait_ge(pre_done, 1)
                act.nop().then_inc(act_done[g], 1)
            with act.Fori(0, CH) as c:
                for g in range(2):
                    b = groups[g]
                    act.wait_ge(dve_done[g], c * len(DVE_S) + 1)
                    lam = chunk_of(lam_all, g, c)
                    A(b["dec"], lam, ACT.Exp).then_inc(act_done[g], 1)
                    A(b["gro"], lam, ACT.Exp, scale=-1.0).then_inc(act_done[g], 1)
                for g in range(2):
                    b = groups[g]
                    wait_dve(act, g, c, "rho")
                    for s, dst in ((0, b["alpha"]), (1, b["rho"])):
                        for h in range(2):
                            r = slice(h * L, (h + 1) * L)
                            A(dst[r, :, h, :], b["ar"][r, :, s, :], ACT.Copy).then_inc(act_done[g], 1)
                bs = lambda g, i: ps[4 * g + i][:].rearrange("p (q h t) -> p q h t", q=GP, h=2)
                half_bank = lambda g, i: ps[4 * g + i][:, 0:GP * L].rearrange("p (q t) -> p q t", q=GP)
                for g in range(2):
                    b = groups[g]
                    wait_pe(act, g, c, "betaT")
                    A(b["bt"], bs(g, 2), ACT.Copy, scale=-1.0).then_inc(act_done[g], 1)
                    wait_pe(act, g, c, "kappaT")
                    A(b["kt"], bs(g, 3), ACT.Copy).then_inc(act_done[g], 1)
                for g in range(2):
                    wait_pe(act, g, c, "y0")
                    A(groups[g]["Y"], bs(g, 0), ACT.Copy).then_inc(act_done[g], 1)
                for i in range(4):
                    for g in range(2):
                        wait_pe(act, g, c, f"t{i + 1}" if i else "y1")
                        A(groups[g]["X"], bs(g, 1), ACT.Copy).then_inc(act_done[g], 1)
                for g in range(2):
                    wait_pe(act, g, c, "t5")
                    A(groups[g]["Y"], bs(g, 2), ACT.Copy).then_inc(act_done[g], 1)
                for g in range(2):
                    wait_pe(act, g, c, "rhs")
                    A(groups[g]["rhs"], half_bank(g, 0), ACT.Copy).then_inc(act_done[g], 1)
                for g in range(2):
                    wait_pe(act, g, c, "u")
                    A(groups[g]["u"], half_bank(g, 1), ACT.Copy).then_inc(act_done[g], 1)
                for g in range(2):
                    wait_pe(act, g, c, "o")
                    A(chunk_of(r_all, g, c), half_bank(g, 2), ACT.Copy).then_inc(act_done[g], 1)

            act.wait_ge(centred, 1)
            A(region(1), r_all, ACT.Square).then_inc(gn_sq, 1)
            act.wait_ge(gvar_ready, 1)
            A(gst[:], gst[:], ACT.Sqrt).then_inc(gstd_ready, 1)
            for p in range(PAIRS):
                for half in range(2):
                    if (2 * p + half) % 2 == 0:
                        unstacks(act, lambda o, i: A(o, i, ACT.Copy), p, half)

            for l in range(2):
                if l == 1:
                    norm_squares(3)
                    act.wait_ge(angles_ready, 1)
                    A(sinn, ang[0].rearrange("p (t j) -> p t j", t=TT), ACT.Sin)
                    A(cosn, ang[1].rearrange("p (t j) -> p t j", t=TT), ACT.Sin).then_inc(sines_ready, 1)
                    norm_out(3, "ln_mix1")
                    for half in range(2):
                        for t in range(TT):
                            name = ("mv", half, t)
                            wait_filled(act, name)
                            empties(A(vm[:, t, half * HB:(half + 1) * HB], bank(name)[:], ACT.Copy), name)
                    for p in range(KT):
                        wait_filled(act, ("mqT", p))
                        empties(A(qmT[:, p], bank(("mqT", p))[:], ACT.Copy), ("mqT", p))
                    for p in range(KT):
                        wait_filled(act, ("mkT", p))
                        empties(A(kmT[:, p], bank(("mkT", p))[:], ACT.Copy), ("mkT", p))

                    def exps(h):
                        for q in range(TT):
                            act.wait_ge(mmax_ready, 4 * h + q + 1)
                            if h >= 2 and q == 0:
                                wait_filled(act, ("mp", h - 2, TT - 1))
                                wait_emptied(act, ("mo", h - 2))
                            w = (q + 1) * P
                            empties(A(pm[:, h % 2, q, 0:w], bank(("ms", h, q))[:, 0:w], ACT.Exp, scale=1 / 8,
                                      bias=nmax[:, h % 2, q:q + 1], accum_out=esum[:, h % 2, q:q + 1]), ("ms", h, q))

                    exps(0)
                    for h in range(NH):
                        if h + 1 < NH:
                            exps(h + 1)
                        for q in range(TT):
                            name = ("mp", h, q)
                            w = (q + 1) * P
                            wait_filled(act, name)
                            empties(A(pmT[:, h % 2, q, 0:w], bank(name)[:, 0:w], ACT.Copy), name)
                    for k in range(0, KT, 2):
                        wait_filled(act, ("moT", k))
                        empties(A(HT[:, k], bank(("moT", k))[:], ACT.Copy), ("moT", k))
                act.wait_ge(mem_loaded, 16 * (l + 1))
                if l == 0:
                    for m in range(MT):
                        A(memT.rearrange("p k m -> p (k m)")[:, m * C:(m + 1) * C], memn[:, m], ACT.Square,
                          accum_out=mss[:, m:m + 1]).then_inc(mem_sq, 1)
                    act.wait_ge(mvar_ready, 1)
                    A(mrstd[:], mss[:], ACT.Sqrt).then_inc(mstd_ready, 1)
                norm_squares(NORM_MEM[l])
                for k in range(KT):
                    wait_filled(act, ("xk", l, k))
                    empties(A(kxT[:, k], bank(("xk", l, k))[:, 0:M], ACT.Copy), ("xk", l, k))
                norm_out(NORM_MEM[l], f"ln_mem{l}")
                for k in range(KT):
                    wait_filled(act, ("xq", l, k))
                    empties(A(qxT[:, k], bank(("xq", l, k))[:], ACT.Copy), ("xq", l, k))

                def xexps(h):
                    for i in range(2):
                        act.wait_ge(xmax_ready, 8 * l + 2 * h + i + 1)
                        if h >= 2 and i == 0:
                            wait_filled(act, ("xp", l, h - 2, MT - 1))
                        name = ("xs", l, h, i)
                        for s in range(2):
                            q = 2 * i + s
                            ins = A(px[:, h % 2, q], bank(name)[:, s * M:(s + 1) * M], ACT.Exp, scale=1 / 16,
                                    bias=nmax[:, h % 2, q:q + 1], accum_out=esum[:, h % 2, q:q + 1])
                        empties(ins, name)

                xexps(0)
                for h in range(XH):
                    if h + 1 < XH:
                        xexps(h + 1)
                    name = ("xp", l, h, 0)
                    wait_filled(act, name)
                    empties(A(pxT[:, h % 2, 0], bank(name)[:], ACT.Copy), name)
                    name = ("xo", l, h, 0)
                    wait_filled(act, name)
                    empties(A(oxT[:, 2 * h], bank(name)[:], ACT.Copy), name)
                norm_squares(NORM_FFN[l])
                norm_out(NORM_FFN[l], f"ln_ffn{l}")
                act.wait_ge(picks_ready, l + 1)
                A(e2[:], e2[:], ACT.Exp).then_inc(gates_exp, 1)

                act.wait_ge(items_ready, l + 1)
                count = act.value_load(item_i[0:1, NBP:NBP + 1], min_val=0, max_val=NB)
                yd = y_rows[l].rearrange("(a b) c -> a b c", b=BR)
                act.wait_ge(y_zeroed, 32)
                for _ in range(PRE):
                    act.nop().then_inc(y_act[l], 1)
                for b in range(2):
                    act.nop().then_inc(y_stored[l][b], 16)

                def tanh(b, number):
                    act.wait_ge(up_done[l], number + 1 + PRE)
                    A(th[b], ps[2 + b][:, 0:256].rearrange("p (f j) -> p f j", f=FT), ACT.Tanh, scale=0.5
                      ).then_inc(th_done[l], 1)

                tanh(0, 0)
                with act.Fori(0, NBP // 2) as i:
                    for b in range(2):
                        with act.If(count > i * 2 + b + 1):
                            tanh(1 - b, i * 2 + b + 1)
                        with act.If(count > i * 2 + b):
                            act.wait_ge(y_stored[l][b], i * 16 + 16)
                            act.wait_ge(down_done[l], i * 2 + b + 1 + PRE)
                            A(y[b][:, 0:HB], ps[4][0:BR, :], ACT.Copy).then_inc(y_act[l], 1)
                            act.wait_ge(y_act[l], i * 2 + b + 1 + PRE)
                            act.wait_ge(y_dve[l], i * 2 + b + 1 + PRE)
                            act.dma_start(yd[bass.ds(i * 2 + b, 1)].rearrange("a b c -> (a b) c"), y[b]
                                          ).then_inc(y_stored[l][b], 16)
                for b in range(2):
                    act.wait_ge(y_stored[l][b], (count + (1 - b)) // 2 * 16 + 16)
                A(gst[0:1, 0:1], ones[0:1, 0:1], ACT.Copy).then_inc(all_stored, 1)
            norm_squares(6)

        @block.vector
        def _(dve):
            V = nc.vector
            n = [0]

            def link(ins):
                n[0] += 1
                ins.then_inc(dve_chain, 1)
                dve.wait_ge(dve_chain, n[0])

            def norm_scale(norm):
                dve.wait_ge(squares_done, 4 * norm + 4)
                V.tensor_scalar(ss[:], ss[:], 1.0 / C, RMS_EPS, ALU.mult, ALU.add).then_inc(var_ready, 1)
                dve.wait_ge(std_ready, norm + 1)
                link(V.reciprocal(rstd[:], rstd[:]))
                for t in range(TT):
                    V.tensor_scalar(XN[:, t], x[:, t], rstd[:, t:t + 1], None, ALU.mult).then_inc(xn_ready, 1)

            def norm_out(norm, gain):
                for k in range(1, KT, 2):
                    name = ("norm", norm, k)
                    wait_filled(dve, name)
                    empties(V.tensor_scalar(HT[:, k], bank(name)[:], col(gain, k), None, ALU.mult), name)

            def add_out(name, half, t):
                wait_filled(dve, name)
                d = x[:, t, half * HB:(half + 1) * HB]
                empties(V.tensor_tensor(d, bank(name)[:], d, ALU.add), name)

            wait_filled(dve, ("params",))
            nr = len(LN) * KT
            V.tensor_copy(par[:, 0:nr], bank(("params",))[:, 0:nr])
            link(V.tensor_copy(par[:, nr:], bank(("params",))[:, nr:nr + len(RW) * KT]))
            link(V.tensor_scalar(half_w0a0[:], par[:, COL["w0"]:COL["w0"] + 2 * KT], 0.5, None, ALU.mult))
            empties(V.tensor_scalar(one_minus_ka[:], par[:, COL["ka"]:COL["ka"] + KT], -1.0, 1.0, ALU.mult, ALU.add),
                    ("params",))
            norm_scale(0)
            norm_out(0, "ln_mix0")
            wait_filled(dve, ("norm", 0, KT - 1))
            for k in range(0, KT, 2):
                wait_emptied(dve, ("norm", 0, k))
                wait_emptied(dve, ("norm", 0, k + 1))
            dx = tiles(region(1), KT)
            V.tensor_scalar(dx[:, :, 0:1], HT[:, :, 0:1], -1.0, None, ALU.mult)
            link(V.tensor_tensor(dx[:, :, 1:], HT[:, :, :-1], HT[:, :, 1:], ALU.subtract))

            def mix(s, dst):
                for k in range(KT):
                    V.scalar_tensor_tensor(tiles(dst, KT)[:, k], dx[:, k], col(f"mu{s}", k), HT[:, k], ALU.mult,
                                           ALU.add).then_inc(mixed, 1)

            def decays():
                tmp = tiles(g_all, KT)
                for p in range(KT):
                    wait_emptied(dve, ("decay", p))
                    lam = tiles(lam_all, KT)[:, p]
                    link(V.tensor_scalar(tmp[:, p % 4], lam, -0.5 * DECAY, -0.5 * DECAY, ALU.mult, ALU.add))
                    V.tensor_tensor_scan(lam, keep, tmp[:, p % 4], 0.0, ALU.mult, ALU.add).then_inc(scans_done, 1)

            def rates():
                for p in range(KT):
                    wait_emptied(dve, ("rate", p))
                    a = tiles(ak_all, KT)[:, p]
                    V.tensor_scalar(a, a, 0.5, 0.5, ALU.mult, ALU.add)

            dve.wait_ge(ids_zeroed, 32)
            dve.wait_ge(consts, 2)
            mix(1, R[0])
            mix(4, R[1])
            mix(5, R[2])
            wait_emptied(dve, ("hidden_g",))
            V.tensor_scalar(hid_g, hid_g, 0.5, 0.5, ALU.mult, ALU.add).then_inc(hid_g_ready, 1)
            mix(0, R[0])
            mix(2, R[2])
            decays()
            rates()
            wait_filled(dve, ("gate", 1, TT - 1))
            mix(3, RE)

            name = ("knorm",)
            wait_filled(dve, name)
            empties(V.tensor_scalar(krt[:], bank(name)[:, 0:64], 1e-24, None, ALU.max), name)
            wait_emptied(dve, name)
            V.nop().then_inc(kvar_ready, 1)
            dve.wait_ge(kstd_ready, 1)
            V.reciprocal(krt[:], krt[:]).then_inc(krinv_ready, 1)
            name = ("knorm_t",)
            wait_filled(dve, name)
            empties(V.tensor_copy(krT[:], bank(name)[0:NH, :]), name)
            for p in range(KT):
                kraw, kkn, a = (tiles(r, KT)[:, p] for r in (k_all, kk_all, ak_all))
                name = ("kscale", p)
                wait_filled(dve, name)
                ins = V.scalar_tensor_tensor(kkn, kraw, col("kk", p), bank(name)[:], ALU.mult, ALU.mult)
                empties(ins, name)
                tmp = tiles(region(1), KT)[:, p]
                link(V.tensor_scalar(tmp, a, col("ka", p), one_minus_ka[:, p:p + 1], ALU.mult, ALU.add))
                link(V.tensor_tensor(kraw, kraw, tmp, ALU.mult))
                wait_emptied(dve, name)
                V.tensor_tensor(a, kkn, a, ALU.mult)
                V.scalar_tensor_tensor(tmp, tiles(r_all, KT)[:, p], col("rk", p), kraw, ALU.mult, ALU.mult
                                       ).then_inc(prod_ready, 1)
            name = ("bonus",)
            wait_filled(dve, name)
            src = bank(name)[:, 0:64].rearrange("p (t q h) -> p q t h", t=TT, q=PAIRS)
            d = bonus[:].rearrange("p q (t e) -> p q t e", e=2)
            for even in range(2):
                for hh in range(2):
                    last = V.tensor_copy(d[hh * 64:hh * 64 + 64, :, :, even], src[even * 64:even * 64 + 64, :, :, hh])
            empties(last, name)

            wait_filled(dve, ("v", 1, TT - 1))
            for g in range(2):
                b = groups[g]
                for m in (b["alpha"], b["rho"], b["beta"], b["kappa"]):
                    V.memset(m.rearrange("p q h t -> p (q h t)"), 0.0)
                link(V.memset(b["S"].rearrange("p q t -> p (q t)"), 0.0))
            V.nop().then_inc(pre_done, 1)
            for g in range(2):
                V.nop().then_inc(dve_done[g], 1)
            bs = lambda g, i: ps[4 * g + i][:].rearrange("p (q h t) -> p q h t", q=GP, h=2)
            half_bank = lambda g, i: ps[4 * g + i][:, 0:GP * L].rearrange("p (q t) -> p q t", q=GP)
            with dve.Fori(0, CH) as c:
                for g in range(2):
                    b = groups[g]
                    kk, ak, kc, rc = (chunk_of(r, g, c) for r in (kk_all, ak_all, k_all, r_all))
                    wait_act(dve, g, c, "decay")
                    V.tensor_tensor(b["ar"][:, :, 0, 1:], kk[:, :, 1:], b["dec"][:, :, :-1], ALU.mult).then_inc(dve_done[g], 1)
                    V.tensor_copy(b["ar"][:, :, 0, 0:1], kk[:, :, 0:1]).then_inc(dve_done[g], 1)
                    V.tensor_tensor(b["ar"][:, :, 1, :], rc, b["dec"], ALU.mult).then_inc(dve_done[g], 1)
                    wait_act(dve, g, c, "growth")
                    for src, dst in ((ak, b["beta"]), (kc, b["kappa"])):
                        for h in range(2):
                            r = slice(h * L, (h + 1) * L)
                            V.tensor_tensor(dst[r, :, h, :], src[r], b["gro"][r], ALU.mult).then_inc(dve_done[g], 1)
                for g in range(2):
                    b = groups[g]
                    col_of = lambda i, s: (ps[4 * g + i][:].rearrange("p (q s t) -> p q s t", q=GP, s=2)[:, :, s, :]
                                           .unsqueeze(2).to_broadcast([P, GP, 2, L]))
                    strict, incl, minus_strict, minus_incl = (
                        m.unsqueeze(1).to_broadcast([P, GP, 2, L]) for m in
                        (m_strict[:], m_incl[:], m_minus[:, 0], m_minus[:, 1]))
                    eye = ident[:].rearrange("p (h t) -> p h t", h=2).unsqueeze(1).to_broadcast([P, GP, 2, L])
                    wait_pe(dve, g, c, "gram_b")
                    V.tensor_tensor(b["X"], col_of(0, 0), minus_strict, ALU.mult).then_inc(dve_done[g], 1)
                    wait_dve(dve, g, c, "x0")
                    V.tensor_tensor(b["Tm"], b["X"], eye, ALU.add).then_inc(dve_done[g], 1)
                    V.tensor_tensor(b["Bn"], col_of(0, 1), minus_incl, ALU.mult).then_inc(dve_done[g], 1)
                    wait_pe(dve, g, c, "gram_k")
                    V.tensor_tensor(b["N"], col_of(1, 0), strict, ALU.mult).then_inc(dve_done[g], 1)
                    V.tensor_tensor(b["K"], col_of(1, 1), incl, ALU.mult).then_inc(dve_done[g], 1)
                for i in range(6):
                    for g in range(2):
                        b = groups[g]
                        if i < 4:
                            wait_pe(dve, g, c, f"t{i + 1}" if i else "y1")
                            V.tensor_copy(b["Y"], bs(g, 2)).then_inc(dve_done[g], 1)
                        if i:
                            wait_pe(dve, g, c, f"t{i + 1}")
                            V.tensor_tensor(b["Tm"], bs(g, 3), b["Tm"], ALU.add).then_inc(dve_done[g], 1)
                for g in range(2):
                    b = groups[g]
                    wait_pe(dve, g, c, "s")
                    V.tensor_tensor(b["S"], half_bank(g, 3), b["S"], ALU.add).then_inc(dve_done[g], 1)
                    wait_dve(dve, g, c, "s_add")
                    V.tensor_tensor(b["S"], b["S"], b["dec"][:, :, L - 1:L].to_broadcast([P, GP, L]), ALU.mult
                                    ).then_inc(dve_done[g], 1)

            for g in range(2):
                dve.wait_ge(act_done[g], 1 + CH * len(ACT_S))
                dve.wait_ge(pe_done[g], 1 + CH * len(PE_S))
            o = r_all.rearrange("p (a v) -> p a v", v=L)
            link(V.tensor_reduce(gst[:], o, AX, ALU.add))
            link(V.tensor_scalar(gst[:], gst[:], 1.0 / L, None, ALU.mult))
            V.tensor_tensor(o, o, gst[:].unsqueeze(2).to_broadcast([P, 64, L]), ALU.subtract).then_inc(centred, 1)
            dve.wait_ge(gn_sq, 1)
            link(V.tensor_reduce(gst[:], region(1).rearrange("p (a v) -> p a v", v=L), AX, ALU.add))
            V.tensor_scalar(gst[:], gst[:], 1.0 / L, GN_EPS, ALU.mult, ALU.add).then_inc(gvar_ready, 1)
            dve.wait_ge(gstd_ready, 1)
            link(V.reciprocal(gst[:], gst[:]))
            link(V.tensor_tensor(o, o, gst[:].unsqueeze(2).to_broadcast([P, 64, L]), ALU.mult))
            dve.wait_ge(lnx_loaded, 64)
            o4 = by_chunk(r_all)
            lnx = [RE[:, i * 512:(i + 1) * 512].rearrange("p (q v) -> p q v", q=PAIRS) for i in range(2)]
            link(V.tensor_tensor(o4, o4, lnx[0].unsqueeze(2).to_broadcast([P, PAIRS, CH, L]), ALU.mult))
            link(V.tensor_tensor(o4, o4, lnx[1].unsqueeze(2).to_broadcast([P, PAIRS, CH, L]), ALU.add))
            v4 = by_chunk(v_all)
            t4 = by_chunk(region(1))
            link(V.tensor_tensor(t4, v4, bonus[:].unsqueeze(3).to_broadcast([P, PAIRS, CH, L]), ALU.mult))
            link(V.tensor_tensor(r_all, r_all, region(1), ALU.add))
            V.tensor_tensor(r_all, r_all, g_all, ALU.mult).then_inc(gn_done, 1)
            for p in range(PAIRS):
                for half in range(2):
                    if (2 * p + half) % 2 == 1:
                        unstacks(dve, V.tensor_copy, p, half)
            for half in range(2):
                for t in range(TT):
                    add_out(("rwkv_out", half, t), half, t)

            for l in range(2):
                if l == 1:
                    norm_scale(3)
                    dve.wait_ge(pos_loaded, 16)
                    link(V.tensor_copy(posf[:], posi[:]))
                    a0, a1, a2, a3 = ang
                    g3 = lambda a: a.rearrange("p (t j) -> p t j", t=TT)
                    link(V.tensor_tensor(g3(a0), posf[:].unsqueeze(2).to_broadcast([P, TT, 32]),
                                         inv_freq[:].unsqueeze(1).to_broadcast([P, TT, 32]), ALU.mult))
                    link(V.tensor_scalar(a1, a0, 1 / (2 * math.pi), ROUND_MAGIC, ALU.mult, ALU.add))
                    link(V.tensor_scalar(a1, a1, ROUND_MAGIC, None, ALU.subtract))
                    for part in TWO_PI_PARTS:
                        link(V.scalar_tensor_tensor(a0, a1, -part, a0, ALU.mult, ALU.add))
                    link(V.tensor_scalar(a0, a0, PI_BELOW, -PI_BELOW, ALU.min, ALU.max))
                    link(V.tensor_scalar(a2, a0, -1.0, None, ALU.mult))
                    link(V.tensor_tensor(a2, a2, a0, ALU.max))
                    V.tensor_scalar(a1, a2, -1.0, math.pi / 2, ALU.mult, ALU.add).then_inc(angles_ready, 1)
                    norm_out(3, "ln_mix1")
                    dve.wait_ge(sines_ready, 1)
                    u = 0
                    for stage, dst in (("mq", qm), ("mk", km)):
                        for half in range(2):
                            for t in range(TT):
                                name = (stage, half, t)
                                wait_filled(dve, name)
                                src = bank(name)[:].rearrange("p (h j) -> p h j", j=32)
                                cs = cosn[:, t].unsqueeze(1).to_broadcast([P, 16, 32])
                                sn = sinn[:, t].unsqueeze(1).to_broadcast([P, 16, 32])
                                A_, B_ = (rot[:, u % 4, i].rearrange("p (h j) -> p h j", j=32) for i in range(2))
                                V.tensor_tensor(A_, src, cs, ALU.mult)
                                ins = V.tensor_tensor(B_, src, sn, ALU.mult)
                                empties(ins, name)
                                wait_emptied(dve, name)
                                A4, B4, D4 = (v.rearrange("p (h s) j -> p h s j", s=2) for v in
                                              (A_, B_, dst[:, t, half * HB:(half + 1) * HB]
                                               .rearrange("p (h j) -> p h j", j=32)))
                                V.tensor_tensor(D4[:, :, 0], A4[:, :, 0], B4[:, :, 1], ALU.subtract)
                                V.tensor_tensor(D4[:, :, 1], A4[:, :, 1], B4[:, :, 0], ALU.add).then_inc(rotated, 1)
                                u += 1

                    def maxes(h):
                        for q in range(TT):
                            name = ("ms", h, q)
                            s = bank(name)
                            wait_filled(dve, name)
                            if h >= 2 and q == 0:
                                wait_emptied(dve, ("ms", h - 2, TT - 1))
                            diag = s[:, q * P:(q + 1) * P]
                            link(V.tensor_tensor(diag, diag, m_causal[:], ALU.add))
                            link(V.tensor_reduce(nmax[:, h % 2, q:q + 1], s[:, 0:(q + 1) * P], AX, ALU.max))
                            V.tensor_scalar(nmax[:, h % 2, q:q + 1], nmax[:, h % 2, q:q + 1], -1 / 8, None, ALU.mult
                                            ).then_inc(mmax_ready, 1)

                    maxes(0)
                    for h in range(NH):
                        if h + 1 < NH:
                            maxes(h + 1)
                        wait_emptied(dve, ("ms", h, TT - 1))
                        for q in range(TT):
                            wait_emptied(dve, ("ms", h, q))
                        link(V.reciprocal(einv[:, h % 2, 0:TT], esum[:, h % 2, 0:TT]))
                        name = ("mo", h)
                        wait_filled(dve, name)
                        src = bank(name)[:, 0:TT * L].rearrange("p (q v) -> p q v", q=TT)
                        empties(V.tensor_tensor(qm[:, :, h * L:(h + 1) * L], src,
                                                einv[:, h % 2, 0:TT].unsqueeze(2).to_broadcast([P, TT, L]), ALU.mult),
                                name)
                    for k in range(1, KT, 2):
                        wait_filled(dve, ("moT", k))
                        empties(V.tensor_copy(HT[:, k], bank(("moT", k))[:]), ("moT", k))
                    for half in range(2):
                        for t in range(TT):
                            add_out(("moba_out", half, t), half, t)
                dve.wait_ge(mem_loaded, 16 * (l + 1))
                if l == 0:
                    dve.wait_ge(mem_sq, MT)
                    V.tensor_scalar(mss[:], mss[:], 1.0 / C, RMS_EPS, ALU.mult, ALU.add).then_inc(mvar_ready, 1)
                    dve.wait_ge(mstd_ready, 1)
                    link(V.reciprocal(mrstd[:], mrstd[:]))
                for m in range(MT):
                    V.tensor_scalar(memn[:, m], memn[:, m], mrstd[:, m:m + 1], None, ALU.mult).then_inc(memn_ready, 1)
                for i in range(KT // 2):
                    name = ("memT", l, i)
                    wait_filled(dve, name)
                    for s in range(2):
                        k = 2 * i + s
                        ins = V.tensor_scalar(memT[:, k], bank(name)[:, s * M:(s + 1) * M], col(f"ln_kv{l}", k), None,
                                              ALU.mult)
                    empties(ins, name)
                norm_scale(NORM_MEM[l])
                for half in range(2):
                    for m in range(MT):
                        name = ("xv", l, half, m)
                        wait_filled(dve, name)
                        empties(V.tensor_copy(vx[:, m, half * HB:(half + 1) * HB], bank(name)[:]), name)
                norm_out(NORM_MEM[l], f"ln_mem{l}")

                def xmaxes(h):
                    for i in range(2):
                        name = ("xs", l, h, i)
                        wait_filled(dve, name)
                        if h >= 2 and i == 0:
                            dve.wait_ge(xprob_ready, 16 * l + 4 * (h - 2) + 4)
                        nm = nmax[:, h % 2, 2 * i:2 * i + 2]
                        link(V.tensor_reduce(nm, bank(name)[:].rearrange("p (s m) -> p s m", s=2), AX, ALU.max))
                        V.tensor_scalar(nm, nm, -1 / 16, None, ALU.mult).then_inc(xmax_ready, 1)

                xmaxes(0)
                for h in range(XH):
                    if h + 1 < XH:
                        xmaxes(h + 1)
                    for i in range(2):
                        wait_emptied(dve, ("xs", l, h, i))
                        link(V.reciprocal(einv[:, h % 2, 2 * i:2 * i + 2], esum[:, h % 2, 2 * i:2 * i + 2]))
                        for q in (2 * i, 2 * i + 1):
                            V.tensor_scalar(px[:, h % 2, q], px[:, h % 2, q], einv[:, h % 2, q:q + 1], None, ALU.mult
                                            ).then_inc(xprob_ready, 1)
                    name = ("xp", l, h, 1)
                    wait_filled(dve, name)
                    empties(V.tensor_copy(pxT[:, h % 2, 1], bank(name)[:]), name)
                    name = ("xo", l, h, 1)
                    wait_filled(dve, name)
                    empties(V.tensor_copy(oxT[:, 2 * h + 1], bank(name)[:]), name)
                for half in range(2):
                    for t in range(TT):
                        add_out(("xattn_out", l, half, t), half, t)
                norm_scale(NORM_FFN[l])
                norm_out(NORM_FFN[l], f"ln_ffn{l}")

                def bc(a, shape, axis):
                    return a.unsqueeze(axis).to_broadcast(shape)

                def first_of(dst, values, best, width, tmp_):
                    link(V.tensor_tensor(tmp_, values, bc(best, [P, TT, width], 2), ALU.is_lt))
                    link(V.scalar_tensor_tensor(tmp_, tmp_, 1000.0, bc(iota[:, 0:width], [P, TT, width], 1), ALU.mult,
                                                ALU.add))
                    link(V.tensor_reduce(dst, tmp_, AX, ALU.min))

                dve.wait_ge(consts, 2)
                dve.wait_ge(router_loaded, 64 * (l + 1))
                name = ("route", l)
                wait_filled(dve, name)
                ins = V.tensor_tensor(logits, bank(name)[:, 0:TT * 36].rearrange("p (t n) -> p t n", t=TT),
                                      bc(br, [P, TT, 36], 1), ALU.add)
                empties(ins, name)
                wait_emptied(dve, name)
                gl = logits[:, :, 0:G]
                link(V.tensor_reduce(gmax, gl, AX, ALU.max))
                first_of(gidx, gl, gmax, G, t4_)
                link(V.tensor_tensor(g1h, bc(iota[:, 0:G], [P, TT, G], 1), bc(gidx, [P, TT, G], 2), ALU.is_equal))
                link(V.tensor_tensor(prod, logits[:, :, G:].rearrange("p t (g e) -> p t e g", g=G),
                                     bc(g1h, [P, TT, EG, G], 2), ALU.mult))
                link(V.tensor_reduce(sel, prod, AX, ALU.add))
                link(V.tensor_reduce(m1, sel, AX, ALU.max))
                first_of(i1, sel, m1, EG, t8)
                link(V.tensor_tensor(t8, bc(iota[:, 0:EG], [P, TT, EG], 1), bc(i1, [P, TT, EG], 2), ALU.is_equal))
                link(V.scalar_tensor_tensor(sel, t8, NEG, sel, ALU.mult, ALU.add))
                link(V.tensor_reduce(m2, sel, AX, ALU.max))
                first_of(i2, sel, m2, EG, t8)
                link(V.tensor_tensor(e2[:, 0:16].rearrange("p (t g) -> p t g", t=TT), gl, bc(gmax, [P, TT, G], 2),
                                     ALU.subtract))
                V.tensor_tensor(e2[:, 16:20], m2, m1, ALU.subtract).then_inc(picks_ready, 1)
                for o_, i_ in ((o1, i1), (o2, i2)):
                    link(V.scalar_tensor_tensor(i_, gidx, float(EG), i_, ALU.mult, ALU.add))
                    link(V.tensor_tensor(o_, bc(iota, [P, TT, E], 1), bc(i_, [P, TT, E], 2), ALU.is_equal))
                V.tensor_tensor(cnt, o1, o2, ALU.add).then_inc(counts_in, 1)
                dve.wait_ge(gates_exp, l + 1)
                link(V.tensor_reduce(gsum, e2[:, 0:16].rearrange("p (t g) -> p t g", t=TT), AX, ALU.add))
                link(V.scalar_tensor_tensor(gsum, e2[:, 16:20], 1.0, gsum, ALU.add, ALU.mult))
                link(V.reciprocal(gate2[:, 0], gsum))
                link(V.tensor_tensor(gate2[:, 1], gate2[:, 0], e2[:, 16:20], ALU.mult))
                name = ("rank", l)
                wait_filled(dve, name)
                rk_ps = bank(name)[:, 0:5 * E].rearrange("p (t e) -> p t e", e=E)
                link(V.memset(one32, 1.0))
                link(V.tensor_scalar(step8, iota[:, 0:8], float(BR), None, ALU.mult))
                link(V.tensor_copy(rank, rk_ps[:, 0:TT]))
                ins = V.tensor_tensor(t32, bc(rk_ps[:, TT], [P, E, 8], 2), bc(step8, [P, E, 8], 1), ALU.is_gt)
                empties(ins, name)
                wait_emptied(dve, name)
                link(V.tensor_reduce(nblk, t32, AX, ALU.add))
                link(V.tensor_tensor_scan(cum, one32, nblk, 0.0, ALU.mult, ALU.add))
                link(V.tensor_tensor(nblk, cum, nblk, ALU.subtract))
                link(V.scalar_tensor_tensor(rank, bc(nblk, [P, TT, E], 1), float(BR), rank, ALU.mult, ALU.add))
                for k, o_ in enumerate((o1, o2)):
                    link(V.tensor_tensor(o_, o_, rank, ALU.mult))
                    link(V.tensor_reduce(dst2[:, k], o_, AX, ALU.add))
                V.tensor_copy(dest_i[:], dst2).then_inc(dest_ready, 1)
                link(V.tensor_tensor(itemc[0:1], bc(cum[0:1], [1, NBP, E], 1), bc(item_no[:], [1, NBP, E], 2),
                                     ALU.is_le))
                link(V.tensor_reduce(itf[0:1, 0:NBP], itemc[0:1], AX, ALU.add))
                link(V.tensor_scalar(itf[0:1, 0:NBP], itf[0:1, 0:NBP], float(E - 1), None, ALU.min))
                link(V.tensor_copy(itf[0:1, NBP:NBP + 1], cum[0:1, E - 1:E]))
                V.tensor_copy(item_i[:], itf[0:1]).then_inc(items_ready, 1)

                dve.wait_ge(items_ready, l + 1)
                count = dve.value_load(item_i[0:1, NBP:NBP + 1], min_val=0, max_val=NB)
                gain = par[:, COL[f"ln_ffn{l}"]:COL[f"ln_ffn{l}"] + KT].unsqueeze(2).to_broadcast([P, KT, BR])

                def rows_out(b, number):
                    dve.wait_ge(rowsT[l], number + PRE)
                    V.tensor_tensor(hgT[b], ps[b][:].rearrange("p (k j) -> p k j", k=KT), gain, ALU.mult
                                    ).then_inc(rowsT_out[l], 1)

                for _ in range(PRE):
                    dve.nop().then_inc(y_dve[l], 1)
                    dve.nop().then_inc(act_ready[l], 1)

                def gated(b, number):
                    dve.wait_ge(th_done[l], number + 1)
                    u1 = ps[2 + b][:, 0:256].rearrange("p (f j) -> p f j", f=FT)
                    u3 = ps[2 + b][:, 256:512].rearrange("p (f j) -> p f j", f=FT)
                    V.scalar_tensor_tensor(ga[b], th[b], 1.0, u1, ALU.add, ALU.mult).then_inc(a_part[l], 1)
                    dve.wait_ge(a_part[l], number + 1)
                    V.scalar_tensor_tensor(hact[b], ga[b], 0.5, u3, ALU.mult, ALU.mult).then_inc(act_ready[l], 1)

                rows_out(0, 1)
                gated(0, 0)
                rows_out(1, 2)
                with dve.Fori(0, NBP // 2) as i:
                    for b in range(2):
                        with dve.If(count > i * 2 + b + 1):
                            gated(1 - b, i * 2 + b + 1)
                            rows_out(b, i * 2 + b + 3)
                        with dve.If(count > i * 2 + b):
                            dve.wait_ge(y_stored[l][b], i * 16 + 16)
                            dve.wait_ge(down_done[l], i * 2 + b + 1 + PRE)
                            V.tensor_copy(y[b][:, HB:2 * HB], ps[5][0:BR, :]).then_inc(y_dve[l], 1)
                for s in range(8):
                    t, k = s // 2, s % 2
                    dve.wait_ge(combined_loaded[l][s], 16)
                    V.scalar_tensor_tensor(x[:, t], combined[s], gate2[:, k, t:t + 1], x[:, t], ALU.mult, ALU.add
                                           ).then_inc(x_updated, 1)
                    dve.wait_ge(x_updated, 8 * l + s + 1)
            norm_scale(6)
            dve.wait_ge(lnf_loaded, 16)
            dve.wait_ge(xn_ready, 28)
            for t in range(TT):
                V.tensor_tensor(XN[:, t], XN[:, t], R[2][:, 0:C], ALU.mult).then_inc(out_ready, 1)

        @block.tensor
        def _(pe):
            nxt = [0]
            mm = nc.tensor.matmul

            def start(name):
                assert ORDER[nxt[0]] == name, (ORDER[nxt[0]], name)
                g = nxt[0]
                nxt[0] += 1
                if g >= 8:
                    pe.wait_ge(emptied[g % 8], g // 8)
                return ps[g % 8]

            def finish(ins):
                ins.then_inc(filled, 1)

            def weights(stage, half):
                j = load_index(stage, half)
                pe.wait_ge(w_loaded[j % 2], 16 * (j // 2 + 1))
                return W[j % 2]

            def transpose_norm(norm):
                for k in range(KT):
                    d = start(("norm", norm, k))
                    for t in range(TT):
                        if k == 0:
                            pe.wait_ge(xn_ready, 4 * norm + t + 1)
                        ins = nc.tensor.transpose(d[:, t * P:(t + 1) * P], XN[:, t, k * P:(k + 1) * P], ident[:])
                    finish(ins)

            def ht_ready(norm, k):
                wait_emptied(pe, ("norm", norm, k))

            def to_channels(stage, rhs, ready, n=T):
                for j in range(KT):
                    w = weights(stage, j // 4) if j % 4 == 0 else w
                    d = start(stage + (j,))
                    for k in range(KT):
                        if j == 0:
                            ready(k)
                        ins = mm(d[:, 0:n], lhsT=w[:, k, (j % 4) * P:(j % 4 + 1) * P], rhs=rhs[:, k, 0:n],
                                 start=k == 0, stop=k == KT - 1)
                    finish(ins)

            def to_tokens(stage, lhs, ready, nt=TT):
                for half in range(2):
                    w = weights(stage, half)
                    for t in range(nt):
                        d = start(stage + (half, t))
                        for k in range(KT):
                            if half == 0 and t == 0:
                                ready(k)
                            ins = mm(d[:], lhsT=lhs[:, k, t * P:(t + 1) * P], rhs=w[:, k, :], start=k == 0,
                                     stop=k == KT - 1)
                        finish(ins)

            pe.wait_ge(consts, 1)
            pe.wait_ge(params_loaded, 16 * 10)
            d = start(("params",))
            nc.tensor.transpose(d[:, 0:64], prow[0:64, :], ident[0:64, 0:64])
            finish(nc.tensor.transpose(d[:, 64:152], qrow[0:88, :], ident[0:88, 0:88]))
            transpose_norm(0)

            mix_ready = lambda s: (lambda k: pe.wait_ge(mixed, s * KT + k + 1))
            xs = [tiles(R[i], KT) for i in range(3)]
            d = start(("hidden_wa",))
            pe.wait_ge(lora_loaded, 16 * 6)
            for k in range(KT):
                mix_ready(0)(k)
                mm(d[0:64, :], lhsT=lw1[:, k], rhs=xs[0][:, k], start=k == 0, stop=k == KT - 1)
            for k in range(KT):
                mix_ready(1)(k)
                ins = mm(d[64:128, :], lhsT=la1[:, k], rhs=xs[1][:, k], start=k == 0, stop=k == KT - 1)
            finish(ins)
            d = start(("hidden_g",))
            for k in range(KT):
                mix_ready(2)(k)
                ins = mm(d[:], lhsT=lg1[:, k], rhs=xs[2][:, k], start=k == 0, stop=k == KT - 1)
            finish(ins)
            wait_emptied(pe, ("hidden_wa",))
            for p in range(KT):
                finish(mm(start(("decay", p))[:], lhsT=lwa2[0:64, p * P:(p + 1) * P], rhs=hid_wa[0:64, :], start=True,
                          stop=True))
            for p in range(KT):
                finish(mm(start(("rate", p))[:], lhsT=lwa2[64:128, p * P:(p + 1) * P], rhs=hid_wa[64:128, :],
                          start=True, stop=True))
            pe.wait_ge(hid_g_ready, 1)
            for half in range(2):
                for t in range(TT):
                    finish(mm(start(("gate", half, t))[:], lhsT=hid_g[:, t * P:(t + 1) * P],
                              rhs=lg2[:, half * HB:(half + 1) * HB], start=True, stop=True))
            to_channels(("r",), xs[0], mix_ready(3))
            to_channels(("k",), xs[2], mix_ready(4))
            to_tokens(("v",), tiles(RE, KT), mix_ready(5))

            pe.wait_ge(consts, 2)
            d = start(("knorm",))
            for t in range(TT):
                for p in range(KT):
                    pe.wait_ge(kk_sq, p + 1)
                    c0 = (t * KT + p) * 2
                    ins = mm(d[:, c0:c0 + 2], lhsT=tiles(region(1), KT)[:, p, t * P:(t + 1) * P], rhs=pair_sel[:],
                             start=True, stop=True)
            finish(ins)
            pe.wait_ge(krinv_ready, 1)
            d = start(("knorm_t",))
            for t in range(TT):
                ins = nc.tensor.transpose(d[0:NH, t * P:(t + 1) * P], krt[:, t * NH:(t + 1) * NH], ident[:])
            finish(ins)
            wait_emptied(pe, ("knorm_t",))
            for p in range(KT):
                finish(mm(start(("kscale", p))[:], lhsT=head_sel[:, p, :], rhs=krT[:], start=True, stop=True))
            d = start(("bonus",))
            for t in range(TT):
                for p in range(KT):
                    pe.wait_ge(prod_ready, p + 1)
                    c0 = (t * KT + p) * 2
                    ins = mm(d[:, c0:c0 + 2], lhsT=tiles(region(1), KT)[:, p, t * P:(t + 1) * P], rhs=pair_sel[:],
                             start=True, stop=True)
            finish(ins)

            for name in ORDER[nxt[0] - 8:nxt[0]]:
                wait_emptied(pe, name)
            pe.wait_ge(pre_done, 1)
            for g in range(2):
                pe.nop().then_inc(pe_done[g], 1)
            def each_pair(dst, width, *terms):
                for q in range(GP):
                    for i, (lhs, rhs) in enumerate(terms):
                        ins = mm(dst[:, q * width:(q + 1) * width], lhsT=lhs(q), rhs=rhs(q), start=i == 0,
                                 stop=i == len(terms) - 1)
                return ins

            square = lambda m: (lambda q: m[:, q].rearrange("p h t -> p (h t)"))
            thin = lambda m: (lambda q: m[:, q])
            with pe.Fori(0, CH) as c:
                for g in range(2):
                    b, bank4 = groups[g], ps[4 * g:4 * g + 4]
                    wait_dve(pe, g, c, "kappa1")
                    ar = lambda q: b["ar"][:, q].rearrange("p s t -> p (s t)")
                    each_pair(bank4[0], P, (square(b["beta"]), ar)).then_inc(pe_done[g], 1)
                    each_pair(bank4[1], P, (square(b["kappa"]), ar)).then_inc(pe_done[g], 1)
                    for i, m in ((2, b["beta"]), (3, b["kappa"])):
                        for q in range(GP):
                            ins = nc.tensor.transpose(bank4[i][:, q * P:(q + 1) * P], square(m)(q), ident[:])
                        ins.then_inc(pe_done[g], 1)
                for g in range(2):
                    b, bank4 = groups[g], ps[4 * g:4 * g + 4]
                    wait_dve(pe, g, c, "bn")
                    for q in range(GP):
                        ins = nc.tensor.transpose(bank4[0][:, q * P:(q + 1) * P], square(b["X"])(q), ident[:])
                    ins.then_inc(pe_done[g], 1)
                for i in range(6):
                    for g in range(2):
                        b, bank4 = groups[g], ps[4 * g:4 * g + 4]
                        X, Y, Tm = square(b["X"]), square(b["Y"]), square(b["Tm"])
                        if i == 0:
                            wait_act(pe, g, c, "y0")
                            wait_dve(pe, g, c, "k")
                        else:
                            wait_act(pe, g, c, f"x{i}" if i < 5 else "y5")
                            if i < 5:
                                wait_dve(pe, g, c, f"t{i}" if i > 1 else "y1")
                            else:
                                wait_dve(pe, g, c, "t5")
                        if i < 4:
                            each_pair(bank4[1], P, (Y, X)).then_inc(pe_done[g], 1)
                        if i < 5:
                            each_pair(bank4[2], P, (X, Y)).then_inc(pe_done[g], 1)
                        if i:
                            each_pair(bank4[3], P, (Y, Tm)).then_inc(pe_done[g], 1)
                v = lambda g: (lambda q: chunk_of(v_all, g, c)[:, q])
                for g in range(2):
                    b, bank4 = groups[g], ps[4 * g:4 * g + 4]
                    wait_act(pe, g, c, "rho1")
                    each_pair(bank4[0], L, (square(b["N"]), v(g)), (square(b["alpha"]), thin(b["S"]))).then_inc(pe_done[g], 1)
                for g in range(2):
                    b, bank4 = groups[g], ps[4 * g:4 * g + 4]
                    wait_act(pe, g, c, "rhs")
                    wait_dve(pe, g, c, "t6")
                    each_pair(bank4[1], L, (square(b["Tm"]), thin(b["rhs"]))).then_inc(pe_done[g], 1)
                for g in range(2):
                    b, bank4 = groups[g], ps[4 * g:4 * g + 4]
                    wait_act(pe, g, c, "u")
                    each_pair(bank4[2], L, (square(b["rho"]), thin(b["S"])), (square(b["Bn"]), thin(b["u"])),
                              (square(b["K"]), v(g))).then_inc(pe_done[g], 1)
                    each_pair(bank4[3], L, (square(b["bt"]), thin(b["u"])), (square(b["kt"]), v(g))).then_inc(pe_done[g], 1)

            pe.wait_ge(gn_done, 1)
            for p in range(PAIRS):
                for half in range(2):
                    d = start(("gn_t", p, half))
                    for c in range(4):
                        ins = nc.tensor.transpose(d[0:64, c * P:(c + 1) * P], by_chunk(r_all)[:, p, half * 4 + c, :],
                                                  ident[:])
                    finish(ins)

            def gn_ready(k):
                wait_emptied(pe, ("gn_t", k, 0))
                wait_emptied(pe, ("gn_t", k, 1))

            to_tokens(("rwkv_out",), HT, gn_ready)

            for l in range(2):
                if l == 1:
                    transpose_norm(3)
                    for i, s in enumerate(("mq", "mk", "mv")):
                        to_tokens((s,), HT, (lambda k: ht_ready(3, k)) if i == 0 else (lambda k: None))
                    for stage, src, base in (("mqT", qm, 0), ("mkT", km, 8)):
                        for p in range(KT):
                            d = start((stage, p))
                            for t in range(TT):
                                pe.wait_ge(rotated, base + (p // 4) * TT + t + 1)
                                ins = nc.tensor.transpose(d[:, t * P:(t + 1) * P], src[:, t, p * P:(p + 1) * P],
                                                          ident[:])
                            finish(ins)

                    def scores(h):
                        p, r = h // 2, slice((h % 2) * L, (h % 2 + 1) * L)
                        for q in range(TT):
                            d = start(("ms", h, q))
                            if h % 2 == 0 and q == 0:
                                wait_emptied(pe, ("mqT", p))
                                wait_emptied(pe, ("mkT", p))
                            w = (q + 1) * P
                            finish(mm(d[:, 0:w], lhsT=qmT[r, p, q * P:(q + 1) * P], rhs=kmT[r, p, 0:w], start=True,
                                      stop=True))

                    for t in range(2 * TT):
                        wait_emptied(pe, ("mv", t // TT, t % TT))
                    scores(0)
                    for h in range(NH):
                        if h + 1 < NH:
                            scores(h + 1)
                        for q in range(TT):
                            d = start(("mp", h, q))
                            wait_emptied(pe, ("ms", h, q))
                            for j in range(q + 1):
                                ins = nc.tensor.transpose(d[:, j * P:(j + 1) * P], pm[:, h % 2, q, j * P:(j + 1) * P],
                                                          ident[:])
                            finish(ins)
                        d = start(("mo", h))
                        for q in range(TT):
                            wait_emptied(pe, ("mp", h, q))
                            for j in range(q + 1):
                                ins = mm(d[:, q * L:(q + 1) * L], lhsT=pmT[:, h % 2, q, j * P:(j + 1) * P],
                                         rhs=vm[:, j, h * L:(h + 1) * L], start=j == 0, stop=j == q)
                        finish(ins)
                    for k in range(KT):
                        d = start(("moT", k))
                        wait_emptied(pe, ("mo", 2 * k + 1))
                        wait_emptied(pe, ("mo", 2 * k))
                        for t in range(TT):
                            ins = nc.tensor.transpose(d[:, t * P:(t + 1) * P], qm[:, t, k * P:(k + 1) * P], ident[:])
                        finish(ins)
                    to_tokens(("moba_out",), HT, lambda k: wait_emptied(pe, ("moT", k)))

                for i in range(KT // 2):
                    d = start(("memT", l, i))
                    for s in range(2):
                        for m in range(MT):
                            pe.wait_ge(memn_ready, MT * l + m + 1)
                            k = 2 * i + s
                            ins = nc.tensor.transpose(d[:, s * M + m * P:s * M + (m + 1) * P],
                                                      memn[:, m, k * P:(k + 1) * P], ident[:])
                    finish(ins)
                to_channels(("xk", l), memT, lambda k: wait_emptied(pe, ("memT", l, k // 2)), n=M)
                to_tokens(("xv", l), memT, lambda k: None, nt=MT)
                transpose_norm(NORM_MEM[l])
                to_channels(("xq", l), HT, lambda k: ht_ready(NORM_MEM[l], k))

                def xscores(h):
                    for i in range(2):
                        d = start(("xs", l, h, i))
                        if i == 0:
                            for c in (2 * h, 2 * h + 1):
                                wait_emptied(pe, ("xq", l, c))
                                wait_emptied(pe, ("xk", l, c))
                        for s in range(2):
                            q = 2 * i + s
                            for c in range(2):
                                ins = mm(d[:, s * M:(s + 1) * M], lhsT=qxT[:, 2 * h + c, q * P:(q + 1) * P],
                                         rhs=kxT[:, 2 * h + c, :], start=c == 0, stop=c == 1)
                        finish(ins)

                xscores(0)
                for h in range(XH):
                    if h + 1 < XH:
                        xscores(h + 1)
                    for m in range(MT):
                        d = start(("xp", l, h, m))
                        for q in range(TT):
                            pe.wait_ge(xprob_ready, 16 * l + 4 * h + q + 1)
                            ins = nc.tensor.transpose(d[:, q * P:(q + 1) * P], px[:, h % 2, q, m * P:(m + 1) * P],
                                                      ident[:])
                        finish(ins)
                    for c in range(2):
                        d = start(("xo", l, h, c))
                        for m in range(MT):
                            if h == 0 and c == 0:
                                wait_emptied(pe, ("xv", l, 0, m))
                                wait_emptied(pe, ("xv", l, 1, m))
                            wait_emptied(pe, ("xp", l, h, m))
                            ins = mm(d[:], lhsT=vx[:, m, h * XD + c * P:h * XD + (c + 1) * P], rhs=pxT[:, h % 2, m],
                                     start=m == 0, stop=m == MT - 1)
                        finish(ins)
                to_tokens(("xattn_out", l), oxT, lambda k: wait_emptied(pe, ("xo", l, k // 2, k % 2)))

                transpose_norm(NORM_FFN[l])
                pe.wait_ge(router_loaded, 64 * (l + 1))
                d = start(("route", l))
                for t in range(TT):
                    for k in range(KT):
                        if t == 0:
                            ht_ready(NORM_FFN[l], k)
                        ins = mm(d[:, t * 36:(t + 1) * 36], lhsT=HT[:, k, t * P:(t + 1) * P], rhs=wr[:, k, :],
                                 start=k == 0, stop=k == KT - 1)
                finish(ins)
                pe.wait_ge(counts_in, l + 1)
                pe.wait_ge(consts, 2)
                d = start(("rank", l))
                for t in range(TT + 1):
                    for j in range(min(t + 1, TT)):
                        last = j == min(t, TT - 1)
                        ins = mm(d[:, t * E:(t + 1) * E], lhsT=before[:] if j == t else ones[:], rhs=cnt[:, j],
                                 start=j == 0, stop=last)
                finish(ins)

                wait_emptied(pe, ("rank", l))
                for name in ORDER[nxt[0] - 8:nxt[0]]:
                    wait_emptied(pe, name)
                pe.wait_ge(items_ready, l + 1)
                count = pe.value_load(item_i[0:1, NBP:NBP + 1], min_val=0, max_val=NB)

                def rows_in(b):
                    for k in range(KT):
                        ins = nc.tensor.transpose(ps[b][:, k * BR:(k + 1) * BR], hg[b][:, k * P:(k + 1) * P],
                                                  ident[0:BR, 0:BR])
                    ins.then_inc(rowsT[l], 1)

                for _ in range(PRE):
                    pe.nop().then_inc(up_done[l], 1)
                    pe.nop().then_inc(down_done[l], 1)
                    pe.nop().then_inc(rowsT[l], 1)

                def up(b, number, use, next_use):
                    pe.wait_ge(rowsT_out[l], number + 1)
                    pe.wait_ge(act_ready[l], number - 1 + PRE)
                    for s in range(2):
                        w = ew[b][s].rearrange("p (k n) -> p k n", k=KT)
                        pe.wait_ge(e_w[l][3 * b + s], use * 16 + 16)
                        if s == 1:
                            pe.wait_ge(gathered[l][1 - b], next_use * 16 + 16)
                        for f in range(FT):
                            c0 = s * 256 + f * BR
                            for k in range(KT):
                                ins = mm(ps[2 + b][:, c0:c0 + BR], lhsT=w[:, k, f * P:(f + 1) * P],
                                         rhs=hgT[b][:, k], start=k == 0, stop=k == KT - 1)
                    ins.then_inc(up_done[l], 1)
                    rows_in(1 - b)

                pe.wait_ge(gathered[l][0], 16)
                rows_in(0)
                up(0, 0, 0, 0)
                with pe.Fori(0, NBP // 2) as i:
                    for b in range(2):
                        with pe.If(count > i * 2 + b + 1):
                            up(1 - b, i * 2 + b + 1, i + b, i + 1)
                        with pe.If(count > i * 2 + b):
                            w2 = ew[b][2].rearrange("p (k n) -> p k n", k=FT)
                            pe.wait_ge(act_ready[l], i * 2 + b + 1 + PRE)
                            pe.wait_ge(e_w[l][3 * b + 2], i * 16 + 16)
                            pe.wait_ge(y_act[l], i * 2 + b + PRE)
                            pe.wait_ge(y_dve[l], i * 2 + b + PRE)
                            for half in range(2):
                                for f in range(FT):
                                    ins = mm(ps[4 + half][0:BR, :], lhsT=hact[b][:, f],
                                             rhs=w2[:, f, half * HB:(half + 1) * HB], start=f == 0, stop=f == FT - 1)
                            ins.then_inc(down_done[l], 1)


_INS = ["x", "mem", "positions", "ln_mix", "ln_mem", "ln_memkv", "ln_ffn", "rw_mu", "rw_w0", "rw_w1", "rw_w2", "rw_a0",
        "rw_a1", "rw_a2", "rw_g1", "rw_g2", "rw_kk", "rw_ka", "rw_rk", "rw_wrkv", "rw_lnx_g", "rw_lnx_b", "rw_wo",
        "mb_wqkv", "mb_wo", "mx_wq", "mx_wkv", "mx_wo", "moe_wg", "moe_bg", "moe_we", "moe_be", "moe_w1", "moe_w3",
        "moe_w2", "ln_f"]


def kernel(**inputs):
    import numpy as _np
    import concourse.bacc as _bacc
    from concourse import mybir as _mybir
    from concourse.bass_utils import run_bass_kernel_spmd as _run

    nc = _bacc.Bacc("TRN2", target_bir_lowering=False, num_devices=1)
    arrays, args = {}, []
    for name in _INS:
        a = _np.ascontiguousarray(inputs[name])
        arrays[f"in_{name}"] = a
        args.append(nc.dram_tensor(f"in_{name}", a.shape, _mybir.dt.from_np(a.dtype), kind="ExternalInput").ap())
    args.append(nc.dram_tensor("out_0", (1, 512, 1024), _mybir.dt.float32, kind="ExternalOutput").ap())
    trunk(nc, *args)
    r = _run(nc, [arrays], core_ids=[0])
    return r.results[0]["out_0"]
```

```python
import math

import concourse.bass as bass
import numpy as np
from concourse import mybir
from contextlib import ExitStack, nullcontext

F32 = mybir.dt.float32
F32R = mybir.dt.float32r
I32 = mybir.dt.int32
ALU = mybir.AluOpType
ACT = mybir.ActivationFunctionType
AX = mybir.AxisListType.X

P = 128
T, C, M = 512, 1024, 256
KT, TT, MT = C // P, T // P, M // P
L = 64
CH = T // L
PAIRS = KT
NH = C // L
HB = 512
XH, XD = 4, 256
G, EG, E, FF = 4, 8, 32, 512
FT = FF // P
BR = 64
NB = 2 * T // BR + E - 1
NX = 2 * T // BR
PRE = 2
NBP = NB + 1
RMS_EPS, GN_EPS, NEG = 1e-6, 64e-5, -1e30
DECAY = math.exp(-0.5)
TWO_PI_PARTS = (6.28125, 0.0019350051879882812, 3.019916e-07)
ROUND_MAGIC = 1.5 * 2.0 ** 23
PI_BELOW = 3.1415925

LN = ["ln_mix0", "ln_mix1", "ln_mem0", "ln_mem1", "ln_kv0", "ln_kv1", "ln_ffn0", "ln_ffn1"]
RW = ["mu0", "mu1", "mu2", "mu3", "mu4", "mu5", "w0", "a0", "kk", "ka", "rk"]
COL = {n: i * KT for i, n in enumerate(LN + RW)}


KSCALES = (range(0, 3), range(3, 6), range(6, 8), range(0))


def bank_group_order():
    o = [("params",)]
    norm = lambda n: [("norm", n, k) for k in range(KT)]
    both = lambda s: [(s, half, t) for half in range(2) for t in range(TT)]
    per = lambda s, *a: [(s, *a, k) for k in range(KT)]
    o += norm(0) + [("hidden_wa",), ("hidden_g",)] + per("decay") + per("rate") + both("gate")
    o += per("r") + per("k") + [("v", 0, t) for t in range(TT)] + [("knorm",)]
    for t, scaled in enumerate(KSCALES):
        o += [("v", 1, t)] + ([("knorm_t",)] if t == 0 else []) + [("kscale", p) for p in scaled]
    o += [("bonus",)]
    o += [("gn_t", p, half) for p in range(PAIRS) for half in range(2)] + both("rwkv_out")
    n = 1
    for l in range(2):
        if l == 1:
            o += norm(n) + both("mq") + both("mk") + both("mv") + per("mqT") + per("mkT")
            n += 1
            o += [("ms", 0, q) for q in range(TT)]
            for h in range(NH):
                if h + 1 < NH:
                    o += [("ms", h + 1, q) for q in range(TT)]
                o += [("mp", h, q) for q in range(TT)] + ([("mo", h - 1)] if h else [])
            o += [("mo", NH - 1)]
            o += per("moT") + both("moba_out")
        o += [("memT", l, i) for i in range(KT // 2)] + per("xk", l)
        o += [("xv", l, half, m) for half in range(2) for m in range(MT)] + norm(n) + per("xq", l)
        n += 1
        o += [("xs", l, 0, i) for i in range(2)]
        for h in range(XH):
            if h + 1 < XH:
                o += [("xs", l, h + 1, i) for i in range(2)]
            o += ([("xo", l, h - 1, c) for c in range(2)] if h else []) + [("xp", l, h, m) for m in range(MT)]
        o += [("xo", l, XH - 1, c) for c in range(2)]
        o += [("xattn_out", l, half, t) for half in range(2) for t in range(TT)]
        o += norm(n) + [("route", l), ("rank", l)]
        n += 1
    return o


def chunk_steps():
    pe = ["gram_b", "gram_k", "betaT", "kappaT", "y0"]
    for i in range(6):
        pe += ([f"x{i + 1}"] if i < 4 else []) + ([f"y{i + 1}"] if i < 5 else []) + ([f"t{i + 1}"] if i else [])
    pe += ["rhs", "u", "o", "s"]
    act = ["decay", "growth", "alpha0", "alpha1", "rho0", "rho1", "beta", "kappa", "y0"]
    act += [f"x{i + 1}" for i in range(4)] + ["y5", "rhs", "u", "o"]
    dve = ["a_rest", "a_first", "rho", "beta0", "beta1", "kappa0", "kappa1", "x0", "t0", "bn", "n", "k"]
    dve += ["y1", "y2", "y3", "y4"]
    dve.insert(dve.index("y2") + 1, "t2")
    dve.insert(dve.index("y3") + 1, "t3")
    dve.insert(dve.index("y4") + 1, "t4")
    dve += ["t5", "t6", "s_add", "s"]
    return pe, act, dve


def trunk(nc, x_in, mem, positions, ln_mix, ln_mem, ln_memkv, ln_ffn, rw_mu, rw_w0, rw_w1, rw_w2, rw_a0, rw_a1,
          rw_a2, rw_g1, rw_g2, rw_kk, rw_ka, rw_rk, rw_wrkv, rw_lnx_g, rw_lnx_b, rw_wo, mb_wqkv, mb_wo, mx_wq,
          mx_wkv, mx_wo, moe_wg, moe_bg, moe_we, moe_be, moe_w1, moe_w3, moe_w2, ln_f, out, stop=99):
    ctx = ExitStack()
    with ctx:
        def sb(name, shape, dt=F32):
            return ctx.enter_context(nc.sbuf_tensor(name, shape, dt))

        def sem(name):
            return ctx.enter_context(nc.semaphore(name))

        ORDER = bank_group_order()
        WHERE = {name: i for i, name in enumerate(ORDER)}

        big_at = (nc.sbuf_base + 31) // 32 * 32
        big = sb("big", [P, 12 * C * 4])

        def region(i, n=1):
            return big[:, i * 4096:(i + n) * 4096]

        def tiles(r, a):
            return r.rearrange("p (a b) -> p a b", a=a)

        x = tiles(region(0), TT)
        XN = tiles(region(1), TT)
        HT = tiles(region(3), KT)
        W = [tiles(region(4 + i), KT) for i in range(2)]
        R = [region(6 + i) for i in range(6)]
        RE = region(2)
        keep = tiles(R[5], KT)[:, KT - 1]

        ident = sb("ident", [P, P])
        ones = sb("ones", [P, P])
        before = sb("before", [P, P])
        m_strict = sb("m_strict", [P, 2, L])
        m_incl = sb("m_incl", [P, 2, L])
        m_minus = sb("m_minus", [P, 2, 2, L])
        m_causal = sb("m_causal", [P, P])
        pair_sel = sb("pair_sel", [P, 2])
        head_sel = sb("head_sel", [NH, PAIRS, P])
        par = sb("par", [P, (len(LN) + len(RW)) * KT])
        half_w0a0 = sb("half_w0a0", [P, 2 * KT])
        one_minus_ka = sb("one_minus_ka", [P, KT])
        bonus = sb("bonus", [P, PAIRS, CH])
        scratch = sb("scratch", [P, 1024])
        hid_wa, hid_g = scratch[:, 0:T], scratch[:, T:2 * T]
        cosn, sinn = (scratch[:, i * P:(i + 1) * P].rearrange("p (t j) -> p t j", t=TT) for i in range(2))
        ang = [scratch[:, (2 + i) * P:(3 + i) * P] for i in range(4)]
        zero = sb("zero", [P, 256])
        ss = sb("ss", [P, TT])
        rstd = sb("rstd", [P, TT])
        mss = sb("mss", [P, MT])
        mrstd = sb("mrstd", [P, MT])
        nmax = sb("nmax", [P, 2, 8])
        esum = sb("esum", [P, 2, 8])
        einv = sb("einv", [P, 2, 8])
        posi = sb("posi", [P, TT], I32)
        posf = sb("posf", [P, TT])
        inv_freq = sb("inv_freq", [P, 32])
        dest_i = sb("dest_i", [P, 2, TT], I32)
        gate2 = sb("gate2", [P, 2, TT])
        tok_i = sb("tok_i", [P, TT], I32)
        idx = [sb(f"idx{i}", [BR, 1], I32) for i in range(2)]
        item_i = sb("item_i", [1, NX + 1], I32)
        item_no = sb("item_no", [1, NX])
        iota = sb("iota", [P, E])[:]
        krt = sb("krt", [P, TT * NH])
        krT = hid_wa[0:NH, :]
        gst = sb("gst", [P, PAIRS * CH])
        e2 = sb("e2", [P, TT * (G + 1)])

        ps = [ctx.enter_context(nc.psum_tensor(f"ps{i}", [P, HB], F32)) for i in range(8)]

        slot_tok = [nc.dram_tensor(f"slot_tok{l}", (NBP * BR, 1), I32, kind="Internal").ap() for l in range(2)]
        h_rows = [nc.dram_tensor(f"h_rows{l}", (T, C), F32, kind="Internal").ap() for l in range(2)]
        y_rows = [nc.dram_tensor(f"y_rows{l}", (NBP * BR, C), F32, kind="Internal").ap() for l in range(2)]

        lw1 = RE[:, 0:512].rearrange("p (k n) -> p k n", k=KT)
        la1 = RE[:, 512:1024].rearrange("p (k n) -> p k n", k=KT)
        lg1 = RE[:, 1024:2048].rearrange("p (k n) -> p k n", k=KT)
        lwa2 = RE[:, 2048:3072]
        lg2 = RE[:, 3072:4096]
        prow, qrow = W[0][:, 0, 0:P], W[0][:, 1, 0:P]

        filled = sem("filled")
        emptied = [sem(f"emptied{b}") for b in range(8)]
        x_loaded, params_loaded, lora_loaded = sem("x_loaded"), sem("params_loaded"), sem("lora_loaded")
        w_loaded = [sem(f"w_loaded{i}") for i in range(2)]
        consts = sem("consts")
        dve_chain, act_chain, pool_chain = sem("dve_chain"), sem("act_chain"), sem("pool_chain")
        squares_done, var_ready, std_ready, xn_ready = (sem(n) for n in
                                                        ("squares_done", "var_ready", "std_ready", "xn_ready"))
        mixed = sem("mixed")
        tanh_g, hid_g_ready, kk_sq, kvar_ready, kstd_ready, krinv_ready, prod_ready, pre_done = (
            sem(n) for n in ("tanh_g", "hid_g_ready", "kk_sq", "kvar_ready", "kstd_ready", "krinv_ready",
                             "prod_ready", "pre_done"))
        scans_done, act_rwkv = sem("scans_done"), sem("act_rwkv")
        pe_done = [sem(f"pe_done{g}") for g in range(2)]
        act_done = [sem(f"act_done{g}") for g in range(2)]
        dve_done = [sem(f"dve_done{g}") for g in range(2)]
        gates_done, gn_scaled = sem("gates_done"), sem("gn_scaled")
        centred, gn_sq, gvar_ready, gstd_ready, gn_done, lnx_loaded = (
            sem(n) for n in ("centred", "gn_sq", "gvar_ready", "gstd_ready", "gn_done", "lnx_loaded"))
        mem_loaded, mem_sq, mvar_ready, mstd_ready, memn_ready = (
            sem(n) for n in ("mem_loaded", "mem_sq", "mvar_ready", "mstd_ready", "memn_ready"))
        xmax_ready, xexp_done, xprob_ready = sem("xmax_ready"), sem("xexp_done"), sem("xprob_ready")
        pos_loaded, angles_ready, sines_ready = sem("pos_loaded"), sem("angles_ready"), sem("sines_ready")
        rot_products, rotated = sem("rot_products"), sem("rotated")
        mmax_ready, mexp_done, msum_inv = sem("mmax_ready"), sem("mexp_done"), sem("msum_inv")
        router_loaded, ids_zeroed, rows_stored, ids_stored = (
            sem(n) for n in ("router_loaded", "ids_zeroed", "rows_stored", "ids_stored"))
        picks_ready, dest_ready, items_ready = sem("picks_ready"), sem("dest_ready"), sem("items_ready")
        e_w = [[sem(f"expert_w{l}{i}") for i in range(6)] for l in range(2)]
        ids_loaded = [[sem(f"ids_loaded{l}{b}") for b in range(2)] for l in range(2)]
        gathered = [[sem(f"gathered{l}{b}") for b in range(2)] for l in range(2)]
        y_stored = [[sem(f"y_stored{l}{b}") for b in range(2)] for l in range(2)]
        rowsT, rowsT_out, up_done, th_done, act_ready, down_done, y_act, y_dve, a_part = (
            [sem(f"{n}{l}") for l in range(2)] for n in
            ("rowsT", "rowsT_out", "up_done", "th_done", "act_ready", "down_done", "y_act", "y_dve", "a_part"))
        w2_rounded, w2_split = ([sem(f"{n}{l}") for l in range(2)] for n in ("w2_rounded", "w2_split"))
        combined_loaded = [[sem(f"combined_loaded{l}{s}") for s in range(8)] for l in range(2)]
        x_updated = sem("x_updated")
        y_zeroed = sem("y_zeroed")
        all_stored = sem("all_stored")
        counts_in, gates_exp = sem("counts_in"), sem("gates_exp")
        lnf_loaded, out_ready, out_stored = sem("lnf_loaded"), sem("out_ready"), sem("out_stored")
        NORM_MEM, NORM_FFN = [1, 4], [2, 5]

        def wait_filled(eng, name):
            eng.wait_ge(filled, WHERE[name] + 1)

        def wait_emptied(eng, name):
            g = WHERE[name]
            eng.wait_ge(emptied[g % 8], g // 8 + 1)

        def bank(name):
            return ps[WHERE[name] % 8]

        def empties(ins, name):
            ins.then_inc(emptied[WHERE[name] % 8], 1)

        def col(name, k):
            return par[:, COL[name] + k:COL[name] + k + 1]

        GP = PAIRS // 2

        groups = []
        for g in range(2):
            views, end = {}, 0
            for name, size in ([("ar", 2 * GP * L)]
                               + [(m, GP * P) for m in ("alpha", "rho", "beta", "kappa", "X", "Y", "Tm", "N", "K",
                                                        "Bn", "bt", "kt")]
                               + [(m, GP * L) for m in ("rhs", "u", "dec", "gro", "S")]):
                r = region(1 if g == 0 else 4, 2)[:, end:end + size]
                end += size
                if name == "ar":
                    views[name] = r.rearrange("p (q s t) -> p q s t", q=GP, s=2)
                elif size == GP * P:
                    views[name] = r.rearrange("p (q h t) -> p q h t", q=GP, h=2)
                else:
                    views[name] = r.rearrange("p (q t) -> p q t", q=GP)
            groups.append(views)
        r_all, k_all, v_all = R[1], R[0], R[2]
        lam_all, ak_all, g_all, kk_all = R[3], R[4], R[5], region(3)
        by_chunk = lambda r: r.rearrange("p (q c t) -> p q c t", q=PAIRS, c=CH)
        PE_S, ACT_S, DVE_S = chunk_steps()


        def after(done, steps, step, c):
            return c * len(steps) + (steps.index(step) + 2)

        def wait_pe(eng, g, c, step):
            eng.wait_ge(pe_done[g], after(pe_done, PE_S, step, c))

        def wait_act(eng, g, c, step):
            eng.wait_ge(act_done[g], after(act_done, ACT_S, step, c))

        def wait_dve(eng, g, c, step):
            eng.wait_ge(dve_done[g], after(dve_done, DVE_S, step, c))

        def chunk_of(r, g, c):
            return by_chunk(r)[:, g * GP:(g + 1) * GP, bass.ds(c, 1), :].rearrange("p q o t -> p q (o t)")

        qxT = tiles(R[0], KT)
        kxT = R[1][:, 0:2048].rearrange("p (k m) -> p k m", k=KT)
        vx = R[1][:, 2048:4096].rearrange("p (m n) -> p m n", m=MT)
        memT = R[2][:, 0:2048].rearrange("p (k m) -> p k m", k=KT)
        memn = R[2][:, 2048:4096].rearrange("p (m n) -> p m n", m=MT)
        oxT = tiles(R[3], KT)
        px = R[4][:, 0:2048].rearrange("p (b q m) -> p b q m", b=2, q=TT)
        pxT = R[5][:, 0:2048].rearrange("p (b m q) -> p b m q", b=2, m=MT)

        qm, km, vm = (tiles(R[i], TT) for i in range(3))
        qmT, kmT = tiles(R[3], KT), tiles(R[4], KT)
        pm = R[5].rearrange("p (b q k) -> p b q k", b=2, q=TT)
        pmT = RE.rearrange("p (b q k) -> p b q k", b=2, q=TT)
        rot = RE.rearrange("p (b s n) -> p b s n", b=4, s=2)

        ew = [[R[3 * b + i] for i in range(2)] for b in range(2)]
        hg = [RE[0:BR, b * 1024:(b + 1) * 1024] for b in range(2)]
        hgT = [region(3)[:, b * 512:(b + 1) * 512].rearrange("p (k j) -> p k j", k=KT) for b in range(2)]
        th = [region(3)[:, 1024 + b * 256:1280 + b * 256].rearrange("p (f j) -> p f j", f=FT) for b in range(2)]
        ga = [region(3)[:, 1536 + b * 256:1792 + b * 256].rearrange("p (f j) -> p f j", f=FT) for b in range(2)]
        hact = [region(3)[:, 2048 + b * 256:2304 + b * 256].rearrange("p (f j) -> p f j", f=FT) for b in range(2)]
        y = [RE[0:BR, 2048 + b * 1024:3072 + b * 1024] for b in range(2)]

        def parts(name, shape, i, first, dt=F32R):
            return nc.alloc_sbuf_tensor_at(name, shape, dt, offset=big_at + (i * 4096 + first) * 4)

        w2_raw = [parts(f"w2_raw{b}", [P, FT, C], 6 + 3 * b + 2, 0, F32) for b in range(2)]

        w2_hi, w2_lo = (parts(n, [P, FT, C], 4 + i, 0) for i, n in enumerate(("w2_hi", "w2_lo")))
        h_hi, h_lo = ([parts(f"{n}{b}", [P, FT, BR], 3, 2560 + (2 * i + b) * 256) for b in range(2)]
                      for i, n in enumerate(("h_hi", "h_lo")))
        wr = RE[:, 0:KT * 36].rearrange("p (k n) -> p k n", k=KT)
        br = RE[:, 288:324]
        at = [KT * 36 + 36]

        def tmp(*shape):
            size = int(np.prod(shape))
            r = RE[:, at[0]:at[0] + size]
            at[0] += size
            names = "abc"[:len(shape)]
            if len(shape) == 1:
                return r
            return r.rearrange(f"p ({' '.join(names)}) -> p {' '.join(names)}", **dict(zip(names, shape)))

        logits, gmax, gidx, g1h, gsum = tmp(TT, 36), tmp(TT), tmp(TT), tmp(TT, G), tmp(TT)
        t4_, sel, prod = tmp(TT, G), tmp(TT, EG), tmp(TT, EG, G)
        m1, i1, m2, i2, t8 = tmp(TT), tmp(TT), tmp(TT), tmp(TT), tmp(TT, EG)
        o1, o2, cnt, rank, dst2 = tmp(TT, E), tmp(TT, E), tmp(TT, E), tmp(TT, E), tmp(2, TT)
        nblk, cum, one32, t32, step7, extra = tmp(E), tmp(E), tmp(E), tmp(E, 7), tmp(7), tmp(TT, E)
        itemc, itf = tmp(NX, E), tmp(NX + 1)
        assert at[0] <= 4096
        combined = [R[i // 4][:, (i % 4) * C:(i % 4 + 1) * C] for i in range(8)]

        loads = []

        def halves(w, last):
            for half in range(2):
                loads.append((w[:, half * HB:(half + 1) * HB].rearrange("(k p) n -> p k n", p=P), last(half)))

        chan_last = lambda s, *a: (lambda half: (s, *a, 4 * half + 3))
        tok_last = lambda s, *a: (lambda half: (s, *a, half, TT - 1))
        halves(rw_wrkv[0, 0], chan_last("r"))
        halves(rw_wrkv[0, 1], chan_last("k"))
        halves(rw_wrkv[0, 2], tok_last("v"))
        halves(rw_wo[0], tok_last("rwkv_out"))
        for l in range(2):
            if l == 1:
                for i, s in enumerate(("mq", "mk", "mv")):
                    halves(mb_wqkv[0, :, i * C:(i + 1) * C], tok_last(s))
                halves(mb_wo[0], tok_last("moba_out"))
            halves(mx_wkv[l, :, 0:C], chan_last("xk", l))
            halves(mx_wkv[l, :, C:2 * C], lambda half, l=l: ("xv", l, half, MT - 1))
            halves(mx_wq[l], chan_last("xq", l))
            halves(mx_wo[l], tok_last("xattn_out", l))
        USE = {}
        for j, (_, last) in enumerate(loads):
            USE.setdefault(last[:-1] if last[0] in ("r", "k", "xk", "xq") else last[:-1], []).append(j)

        def load_index(stage, half):
            if stage[0] in ("r", "k", "xk", "xq"):
                return USE[stage][half]
            return USE[stage + (half,)][0]

        def unstacks(eng, copy, p, half):
            name = ("gn_t", p, half)
            wait_filled(eng, name)
            src = bank(name)[0:L, :].rearrange("p (c h t) -> p c h t", c=4, h=2)
            for hh in range(2):
                dst = HT[hh * L:(hh + 1) * L, p, half * 256:(half + 1) * 256].rearrange("p (c t) -> p c t", c=4)
                ins = copy(dst, src[:, :, hh, :])
            empties(ins, name)

        def blocks(eng, count):
            sure, usual = E // 2 - 1, E // 2 + 2
            with eng.Fori(0, sure) as i:
                for b in range(2):
                    yield i, b, lambda number: nullcontext()
            for first, end in ((sure, usual), (usual, NBP // 2)):
                with eng.If(count > 2 * first):
                    with eng.Fori(first, end) as i:
                        for b in range(2):
                            yield i, b, lambda number: eng.If(count > number)

        def clear(eng, b):
            for m in (b["alpha"], b["rho"], b["beta"], b["kappa"]):
                eng.memset(m.rearrange("p q h t -> p (q h t)"), 0.0)
            eng.memset(b["S"].rearrange("p q t -> p (q t)"), 0.0).then_inc(pre_done, 1)

        def all_of(r, c):
            return by_chunk(r)[:, :, bass.ds(c, 1), :].rearrange("p q o t -> p q (o t)")

        lnx = [scratch[:, i * 512:(i + 1) * 512].rearrange("p (q v) -> p q v", q=PAIRS) for i in range(2)]
        GS = 4
        sliced = lambda r, i: r[:, i * 4096 // GS:(i + 1) * 4096 // GS]
        block = ctx.enter_context(nc.Block())

        @block.sync
        def _(sp):
            sp.dma_start(x, x_in[0].rearrange("(t p) c -> p t c", p=P)).then_inc(x_loaded, 16)
            sp.dma_start(lw1, rw_w1[0].rearrange("(k p) n -> p k n", p=P)).then_inc(lora_loaded, 16)
            sp.dma_start(la1, rw_a1[0].rearrange("(k p) n -> p k n", p=P)).then_inc(lora_loaded, 16)
            sp.dma_start(lg1, rw_g1[0].rearrange("(k p) n -> p k n", p=P)).then_inc(lora_loaded, 16)
            sp.dma_start(lwa2[0:64, :], rw_w2[0]).then_inc(lora_loaded, 16)
            sp.dma_start(lwa2[64:128, :], rw_a2[0]).then_inc(lora_loaded, 16)
            sp.dma_start(lg2, rw_g2[0]).then_inc(lora_loaded, 16)
            sp.dma_start(posi[:], positions[0].rearrange("(t p) -> p t", p=P), allow_slow_non_contiguous=True).then_inc(pos_loaded, 16)
            wait_emptied(sp, ("params",))

            def load(j):
                if j >= 2:
                    wait_filled(sp, loads[j - 2][1])
                sp.dma_start(W[j % 2], loads[j][0]).then_inc(w_loaded[j % 2], 16)

            def load_mem(l):
                sp.dma_start(memn, mem[0].rearrange("(m p) c -> p m c", p=P)).then_inc(mem_loaded, 16)

            def up_matrices(l, b, e):
                for s, w in ((0, moe_w1), (1, moe_w3)):
                    dst = ew[b][s].rearrange("p (k n) -> p k n", k=KT)
                    src = w[l].rearrange("e (k p) n -> e p k n", p=P)[bass.ds(e, 1)]
                    sp.dma_start(dst, src.rearrange("o p k n -> (o p) k n")).then_inc(e_w[l][3 * b + s], 16)

            def down_matrix(l, b, e):
                dst = w2_raw[b][:]
                src = moe_w2[l].rearrange("e (k p) n -> e p k n", p=P)[bass.ds(e, 1)]
                sp.dma_start(dst, src.rearrange("o p k n -> (o p) k n")).then_inc(e_w[l][3 * b + 2], 16)

            def experts(l):
                sp.wait_ge(items_ready, l + 1)
                count = sp.value_load(item_i[0:1, NX:NX + 1], min_val=0, max_val=NB)

                def expert(i, number):
                    return sp.value_load(item_i[0:1, bass.ds(i * 2 + (number - E), 1)], min_val=0, max_val=E - 1)

                sure, usual = E // 2 - 1, E // 2 + 2
                with sp.Fori(0, sure) as i:
                    for b in range(2):
                        sp.wait_ge(up_done[l], i * 2 + b + 1 + PRE)
                        up_matrices(l, b, i * 2 + b + 2)
                        sp.wait_ge(down_done[l], i * 2 + b + PRE)
                        down_matrix(l, 1 - b, i * 2 + b + 1)
                sp.wait_ge(down_done[l], 2 * sure + PRE)
                down_matrix(l, 1, E - 1)
                for first, end in ((sure, usual), (usual, NBP // 2 - 1)):
                    with sp.If(count > 2 * first + 2):
                        with sp.Fori(first, end) as i:
                            for b in range(2):
                                with sp.If(count > i * 2 + b + 2):
                                    e = expert(i, b + 2)
                                    sp.wait_ge(up_done[l], i * 2 + b + 1 + PRE)
                                    up_matrices(l, b, e)
                                    sp.wait_ge(down_done[l], i * 2 + b + 1 + PRE)
                                    down_matrix(l, b, e)
                return count

            for j in range(6):
                load(j)
            sp.wait_ge(consts, 1)
            for l in range(2):
                sp.dma_start(y_rows[l][E * BR:].rearrange("(p a) (s c) -> p (a s) c", p=P, s=C // 256),
                             zero[:].unsqueeze(1).to_broadcast([P, (NBP - E) * BR // P * (C // 256), 256])
                             ).then_inc(y_zeroed, 16)
            wait_filled(sp, ("kscale", KT - 1))
            for i, v in enumerate((rw_lnx_g, rw_lnx_b)):
                for hh in range(2):
                    sp.dma_start(lnx[i][hh * 64:hh * 64 + 64],
                                 v[0].rearrange("(q h v) -> h q v", q=PAIRS, h=2)[hh].partition_broadcast(64)
                                 ).then_inc(lnx_loaded, 16)
            for g in range(2):
                sp.wait_ge(pe_done[g], 1 + CH * len(PE_S))
                sp.wait_ge(act_done[g], 1 + CH * len(ACT_S))
                sp.wait_ge(dve_done[g], 1 + CH * len(DVE_S))
            load(6)
            load(7)
            sp.wait_ge(gn_done, GS)
            load_mem(0)
            j = 8
            for l in range(2):
                if l == 1:
                    for _ in range(4):
                        load(j)
                        j += 1
                    load(j)
                    load(j + 1)
                    j += 2
                    wait_emptied(sp, ("moT", KT - 1))
                    load_mem(1)
                for _ in range(8):
                    load(j)
                    j += 1
                if l == 1:
                    wait_emptied(sp, ("mo", NH - 1))
                else:
                    sp.wait_ge(gn_done, GS)
                sp.dma_start(wr[:, :, 0:G], moe_wg[l].rearrange("(k p) n -> p k n", p=P)).then_inc(router_loaded, 16)
                sp.dma_start(wr[:, :, G:G + E], moe_we[l].rearrange("(k p) n -> p k n", p=P)).then_inc(router_loaded, 16)
                sp.dma_start(br[:, 0:G], moe_bg[l].partition_broadcast(P)).then_inc(router_loaded, 16)
                sp.dma_start(br[:, G:G + E], moe_be[l].partition_broadcast(P)).then_inc(router_loaded, 16)
                wait_filled(sp, ("xo", l, XH - 1, 1))
                up_matrices(l, 0, 0)
                down_matrix(l, 0, 0)
                wait_filled(sp, ("xattn_out", l, 1, TT - 1))
                up_matrices(l, 1, 1)
                sp.wait_ge(xn_ready, 4 * NORM_FFN[l] + 4)
                sp.dma_start(h_rows[l].rearrange("(t p) c -> p t c", p=P), XN).then_inc(rows_stored, 16)
                count = experts(l)
                if l == 0:
                    sp.wait_ge(down_done[l], count + PRE)
                    sp.wait_ge(combined_loaded[l][7], 16)
                    load(j)
                    load(j + 1)
                    j += 2
            sp.wait_ge(x_updated, 16)
            sp.dma_start(R[2][:, 0:C], ln_f.partition_broadcast(P)).then_inc(lnf_loaded, 16)
            for t in range(TT):
                sp.wait_ge(out_ready, t + 1)
                sp.dma_start(out[0, t * P:(t + 1) * P, :], XN[:, t]).then_inc(out_stored, 16)
            sp.wait_ge(out_stored, 16 * TT)

        @block.gpsimd
        def _(pool):
            n = [0]

            def link(ins):
                n[0] += 1
                ins.then_inc(pool_chain, 1)
                pool.wait_ge(pool_chain, n[0])

            def triangle(out, in_, op, fill, base=0, mult=1, pattern=None):
                return pool.affine_select(out=out, in_=in_, compare_op=op, fill=fill, base=base,
                                          pattern=pattern or [[-1, P]], channel_multiplier=mult)

            link(pool.memset(ident[:], 0.0))
            link(pool.memset(zero[:], 0.0))
            triangle(ident[:], ident[:], ALU.not_equal, 1.0).then_inc(consts, 1)
            link(pool.memset(ones[:], 1.0))
            link(triangle(before[:], ones[:], ALU.is_gt, 0.0, mult=-1, pattern=[[1, P]]))
            flat = lambda m: m[:].rearrange("p h t -> p (h t)")
            link(triangle(flat(m_strict), ones[:], ALU.is_gt, 0.0, mult=-1, pattern=[[1, P]]))
            link(triangle(flat(m_incl), ones[:], ALU.is_ge, 0.0, mult=-1, pattern=[[1, P]]))
            link(pool.memset(m_strict[0:64, 1, :], 0.0))
            link(pool.memset(m_incl[0:64, 1, :], 0.0))
            link(pool.tensor_scalar(m_minus[:, 0], m_strict[:], -1.0, None, ALU.mult))
            link(pool.tensor_scalar(m_minus[:, 1], m_incl[:], -1.0, None, ALU.mult))
            link(pool.memset(m_causal[:], 0.0))
            link(triangle(m_causal[:], m_causal[:], ALU.is_ge, NEG))
            link(pool.memset(pair_sel[:], 0.0))
            link(pool.memset(pair_sel[0:64, 0:1], 1.0))
            link(pool.memset(pair_sel[64:128, 1:2], 1.0))
            link(pool.memset(keep, 1.0))
            link(pool.memset(keep.rearrange("p (c t) -> p c t", t=L)[:, :, 0:1], 0.0))
            link(pool.memset(head_sel[:], 0.0))
            hs = head_sel[:].rearrange("h q (s j) -> h q s j", s=2)
            link(pool.affine_select(out=hs, in_=hs, compare_op=ALU.not_equal, fill=1.0, base=0,
                                    pattern=[[-2, PAIRS], [-1, 2], [0, L]], channel_multiplier=1))
            for j in range(32):
                pool.memset(inv_freq[:, j:j + 1], float(np.float32(10000.0) ** np.float32(-j * 2.0 / 64)))
            link(pool.iota(tok_i[:], [[P, TT]], base=0, channel_multiplier=1))
            link(pool.iota(iota, [[1, E]], base=0, channel_multiplier=0, allow_small_or_imprecise_dtypes=True))
            pool.iota(item_no[:], [[1, NX]], base=0, channel_multiplier=0, allow_small_or_imprecise_dtypes=True
                      ).then_inc(consts, 1)
            zeros = region(6)[0:NBP, 0:BR].bitcast(I32)
            link(pool.memset(zeros, 0))
            for l in range(2):
                pool.dma_start(slot_tok[l].rearrange("(a b) o -> a (b o)", b=BR), zeros).then_inc(ids_zeroed, 16)
            pool.wait_ge(ids_zeroed, 32)
            wait_filled(pool, ("bonus",))
            clear(pool, groups[0])
            wait_emptied(pool, ("bonus",))
            pool.wait_ge(lnx_loaded, 64)
            for c in range(CH):
                for g in range(2):
                    wait_dve(pool, g, c, "kappa1")
                biased, v_c, g_c = (all_of(r, c) for r in (ak_all, v_all, g_all))
                bonus_c = bonus[:, :, bass.ds(c, 1)].to_broadcast([P, PAIRS, L])
                pool.tensor_tensor(biased, v_c, bonus_c, ALU.mult).then_inc(gates_done, 1)
                pool.wait_ge(gates_done, c * 4 + 1)
                pool.tensor_tensor(biased, biased, lnx[1], ALU.add).then_inc(gates_done, 1)
                pool.wait_ge(gates_done, c * 4 + 2)
                pool.tensor_tensor(biased, biased, g_c, ALU.mult).then_inc(gates_done, 1)
                pool.wait_ge(gates_done, c * 4 + 3)
                pool.tensor_tensor(g_c, g_c, lnx[0], ALU.mult).then_inc(gates_done, 1)
            for i in range(GS):
                pool.wait_ge(gn_scaled, i + 1)
                pool.tensor_tensor(sliced(r_all, i), sliced(r_all, i), sliced(ak_all, i), ALU.add).then_inc(gn_done, 1)

            for l in range(2):
                for k in range(2):
                    for t in range(TT):
                        if k == 0 and t == 0:
                            pool.wait_ge(dest_ready, l + 1)
                        pool.indirect_dma_start(
                            slot_tok[l], bass.IndirectOffsetOnAxis(ap=dest_i[:, k, t:t + 1], axis=0),
                            tok_i[:, t:t + 1], None).then_inc(ids_stored, 16)
                pool.wait_ge(ids_stored, 16 * 8 * (l + 1))
                pool.wait_ge(rows_stored, 16 * (l + 1))
                pool.wait_ge(items_ready, l + 1)
                count = pool.value_load(item_i[0:1, NX:NX + 1], min_val=0, max_val=NB)
                ids_of = slot_tok[l].rearrange("(a b) o -> a b o", b=BR)
                def gather(n_block):
                    b = n_block % 2
                    pool.wait_ge(rowsT[l], n_block - 1 + PRE)
                    pool.dma_start(idx[b][:], ids_of[n_block]).then_inc(ids_loaded[l][b], 16)
                    pool.wait_ge(ids_loaded[l][b], 16 * (n_block // 2 + 1))
                    pool.indirect_dma_start(hg[b], None, h_rows[l],
                                            bass.IndirectOffsetOnAxis(ap=idx[b][:], axis=0)
                                            ).then_inc(gathered[l][b], 16)

                for n_block in range(E + 1):
                    gather(n_block)
                for first in range(E + 1, NBP, 5):
                    with pool.If(count + 1 > first):
                        gather(first)
                        for n_block in range(first + 1, min(first + 5, NBP)):
                            with pool.If(count + 1 > n_block):
                                gather(n_block)
                pool.wait_ge(all_stored, l + 1)
                for s in range(8):
                    t, k = s // 2, s % 2
                    pool.indirect_dma_start(combined[s], None, y_rows[l],
                                            bass.IndirectOffsetOnAxis(ap=dest_i[:, k, t:t + 1], axis=0)
                                            ).then_inc(combined_loaded[l][s], 16)

        @block.scalar
        def _(act):
            A = nc.scalar.activation
            n = [0]

            def link(ins):
                n[0] += 1
                ins.then_inc(act_chain, 1)
                act.wait_ge(act_chain, n[0])

            def wait_x(norm, t):
                if norm == 0:
                    act.wait_ge(x_loaded, 16)
                elif norm == 1:
                    wait_emptied(act, ("rwkv_out", 1, t))
                elif norm in (2, 5):
                    wait_emptied(act, ("xattn_out", norm // 3, 1, t))
                elif norm == 3:
                    act.wait_ge(x_updated, 2 * t + 2)
                elif norm == 4:
                    wait_emptied(act, ("moba_out", 1, t))
                else:
                    act.wait_ge(x_updated, 8 + 2 * t + 2)

            def norm_squares(norm):
                for t in range(TT):
                    wait_x(norm, t)
                    A(XN[:, t], x[:, t], ACT.Square, accum_out=ss[:, t:t + 1]).then_inc(squares_done, 1)
                act.wait_ge(var_ready, norm + 1)
                A(rstd[:], ss[:], ACT.Sqrt).then_inc(std_ready, 1)

            def norm_out(norm, gain):
                for k in range(0, KT, 2):
                    name = ("norm", norm, k)
                    wait_filled(act, name)
                    empties(A(HT[:, k], bank(name)[:], ACT.Copy, scale=col(gain, k)), name)

            for i, v in enumerate((ln_mix, ln_mem, ln_memkv, ln_ffn)):
                act.dma_start(prow[16 * i:16 * i + 16, :], v.rearrange("l (k p) -> (l k) p", p=P)
                              ).then_inc(params_loaded, 16)
            act.dma_start(qrow[0:48, :], rw_mu[0].rearrange("s (k p) -> (s k) p", p=P)).then_inc(params_loaded, 16)
            for i, v in enumerate((rw_w0, rw_a0, rw_kk, rw_ka)):
                act.dma_start(qrow[48 + 8 * i:56 + 8 * i, :], v[0].rearrange("(k p) -> k p", p=P)
                              ).then_inc(params_loaded, 16)
            act.dma_start(qrow[80:88, :], rw_rk[0].rearrange("(k h) d -> k (h d)", h=2)).then_inc(params_loaded, 16)

            norm_squares(0)
            norm_out(0, "ln_mix0")
            wait_filled(act, ("hidden_wa",))
            A(hid_wa[0:64, :], bank(("hidden_wa",))[0:64, :], ACT.Tanh)
            empties(A(hid_wa[64:128, :], bank(("hidden_wa",))[64:128, :], ACT.Copy), ("hidden_wa",))
            wait_filled(act, ("hidden_g",))
            empties(A(hid_g, bank(("hidden_g",))[:], ACT.Tanh, scale=0.5), ("hidden_g",))
            for stage, dst, c in (("decay", lam_all, 0), ("rate", ak_all, KT)):
                for p in range(KT):
                    wait_filled(act, (stage, p))
                    empties(A(tiles(dst, KT)[:, p], bank((stage, p))[:], ACT.Tanh, scale=0.5,
                              bias=half_w0a0[:, c + p:c + p + 1]), (stage, p))

            def stack(dst, name, half, t):
                wait_filled(act, name)
                src = bank(name)[:].rearrange("p (q h v) -> p q h v", q=4, h=2)
                d = by_chunk(dst)
                for even in range(2):
                    for hh in range(2):
                        last = A(d[hh * 64:hh * 64 + 64, 4 * half:4 * half + 4, 2 * t + even, :],
                                 src[even * 64:even * 64 + 64, :, hh, :], ACT.Copy)
                empties(last, name)

            act.wait_ge(scans_done, KT)
            for half in range(2):
                for t in range(TT):
                    stack(g_all, ("gate", half, t), half, t)
            for stage, dst in (("r", r_all), ("k", k_all)):
                for p in range(KT):
                    wait_filled(act, (stage, p))
                    empties(A(tiles(dst, KT)[:, p], bank((stage, p))[:], ACT.Copy), (stage, p))
            for p in range(KT):
                wait_emptied(act, ("k", p))
                if p == 0:
                    act.wait_ge(mixed, 6 * KT)
                A(tiles(region(1), KT)[:, p], tiles(k_all, KT)[:, p], ACT.Square, scale=col("kk", p)
                  ).then_inc(kk_sq, 1)
            for half in range(2):
                for t in range(TT):
                    stack(v_all, ("v", half, t), half, t)
                if half == 0:
                    act.wait_ge(kvar_ready, 1)
                    A(krt[:], krt[:], ACT.Sqrt).then_inc(kstd_ready, 1)

            for g in range(2):
                act.wait_ge(pre_done, 2)
                act.nop().then_inc(act_done[g], 1)
            A(gst[0:1, 0:1], ones[0:1, 0:1], ACT.Exp)
            with act.Fori(0, CH) as c:
                for g in range(2):
                    b = groups[g]
                    act.wait_ge(dve_done[g], c * len(DVE_S) + 1)
                    lam = chunk_of(lam_all, g, c)
                    A(b["dec"], lam, ACT.Exp).then_inc(act_done[g], 1)
                    A(b["gro"], lam, ACT.Exp, scale=-1.0).then_inc(act_done[g], 1)
                for g in range(2):
                    b = groups[g]
                    wait_dve(act, g, c, "rho")
                    for s, dst in ((0, b["alpha"]), (1, b["rho"])):
                        for h in range(2):
                            r = slice(h * L, (h + 1) * L)
                            A(dst[r, :, h, :], b["ar"][r, :, s, :], ACT.Copy).then_inc(act_done[g], 1)
                bs = lambda g, i: ps[4 * g + i][:].rearrange("p (q h t) -> p q h t", q=GP, h=2)
                half_bank = lambda g, i: ps[4 * g + i][:, 0:GP * L].rearrange("p (q t) -> p q t", q=GP)
                for g in range(2):
                    b = groups[g]
                    wait_pe(act, g, c, "betaT")
                    A(b["bt"], bs(g, 2), ACT.Copy, scale=-1.0).then_inc(act_done[g], 1)
                    wait_pe(act, g, c, "kappaT")
                    A(b["kt"], bs(g, 3), ACT.Copy).then_inc(act_done[g], 1)
                for g in range(2):
                    wait_pe(act, g, c, "y0")
                    A(groups[g]["Y"], bs(g, 0), ACT.Copy).then_inc(act_done[g], 1)
                for i in range(4):
                    for g in range(2):
                        wait_pe(act, g, c, f"t{i + 1}" if i else "y1")
                        A(groups[g]["X"], bs(g, 1), ACT.Copy).then_inc(act_done[g], 1)
                for g in range(2):
                    wait_pe(act, g, c, "t5")
                    A(groups[g]["Y"], bs(g, 2), ACT.Copy).then_inc(act_done[g], 1)
                for g in range(2):
                    wait_pe(act, g, c, "rhs")
                    A(groups[g]["rhs"], half_bank(g, 0), ACT.Copy).then_inc(act_done[g], 1)
                for g in range(2):
                    wait_pe(act, g, c, "u")
                    A(groups[g]["u"], half_bank(g, 1), ACT.Copy).then_inc(act_done[g], 1)
                for g in range(2):
                    wait_pe(act, g, c, "o")
                    A(chunk_of(r_all, g, c), half_bank(g, 2), ACT.Copy).then_inc(act_done[g], 1)

            for i in range(GS):
                act.wait_ge(centred, i + 1)
                A(sliced(region(1), i), sliced(r_all, i), ACT.Square).then_inc(gn_sq, 1)
            act.wait_ge(gvar_ready, 1)
            A(gst[:], gst[:], ACT.Sqrt).then_inc(gstd_ready, 1)
            for p in range(PAIRS):
                for half in range(2):
                    if (2 * p + half) % 2 == 0:
                        unstacks(act, lambda o, i: A(o, i, ACT.Copy), p, half)

            for l in range(2):
                if l == 1:
                    norm_squares(3)
                    act.wait_ge(angles_ready, 1)
                    A(sinn, ang[0].rearrange("p (t j) -> p t j", t=TT), ACT.Sin)
                    A(cosn, ang[1].rearrange("p (t j) -> p t j", t=TT), ACT.Sin).then_inc(sines_ready, 1)
                    norm_out(3, "ln_mix1")
                    for half in range(2):
                        for t in range(TT):
                            name = ("mv", half, t)
                            wait_filled(act, name)
                            empties(A(vm[:, t, half * HB:(half + 1) * HB], bank(name)[:], ACT.Copy), name)
                    for p in range(KT):
                        wait_filled(act, ("mqT", p))
                        empties(A(qmT[:, p], bank(("mqT", p))[:], ACT.Copy), ("mqT", p))
                    for p in range(KT):
                        wait_filled(act, ("mkT", p))
                        empties(A(kmT[:, p], bank(("mkT", p))[:], ACT.Copy), ("mkT", p))

                    def exp(h, q):
                        act.wait_ge(mmax_ready, 4 * h + q + 1)
                        if h >= 2 and q == 0:
                            wait_filled(act, ("mp", h - 2, TT - 1))
                        w = (q + 1) * P
                        empties(A(pm[:, h % 2, q, 0:w], bank(("ms", h, q))[:, 0:w], ACT.Exp, scale=1 / 8,
                                  bias=nmax[:, h % 2, q:q + 1], accum_out=esum[:, h % 2, q:q + 1]), ("ms", h, q))

                    def transposed(h, q):
                        name = ("mp", h, q)
                        w = (q + 1) * P
                        wait_filled(act, name)
                        empties(A(pmT[:, h % 2, q, 0:w], bank(name)[:, 0:w], ACT.Copy), name)

                    for q in range(TT):
                        exp(0, q)
                    for h in range(NH):
                        for step, q in ((exp, 0), (transposed, 0), (transposed, 1), (exp, 1), (transposed, 2),
                                        (exp, 2), (transposed, 3), (exp, 3)):
                            if step == transposed:
                                transposed(h, q)
                            elif h + 1 < NH:
                                exp(h + 1, q)
                    for k in range(0, KT, 2):
                        wait_filled(act, ("moT", k))
                        empties(A(HT[:, k], bank(("moT", k))[:], ACT.Copy), ("moT", k))
                act.wait_ge(mem_loaded, 16 * (l + 1))
                if l == 0:
                    for m in range(MT):
                        A(memT.rearrange("p k m -> p (k m)")[:, m * C:(m + 1) * C], memn[:, m], ACT.Square,
                          accum_out=mss[:, m:m + 1]).then_inc(mem_sq, 1)
                    act.wait_ge(mvar_ready, 1)
                    A(mrstd[:], mss[:], ACT.Sqrt).then_inc(mstd_ready, 1)
                norm_squares(NORM_MEM[l])
                for k in range(KT):
                    wait_filled(act, ("xk", l, k))
                    empties(A(kxT[:, k], bank(("xk", l, k))[:, 0:M], ACT.Copy), ("xk", l, k))
                norm_out(NORM_MEM[l], f"ln_mem{l}")
                for k in range(KT):
                    wait_filled(act, ("xq", l, k))
                    empties(A(qxT[:, k], bank(("xq", l, k))[:], ACT.Copy), ("xq", l, k))

                def xexps(h):
                    for i in range(2):
                        act.wait_ge(xmax_ready, 8 * l + 2 * h + i + 1)
                        if h >= 2 and i == 0:
                            wait_filled(act, ("xp", l, h - 2, MT - 1))
                        name = ("xs", l, h, i)
                        for s in range(2):
                            q = 2 * i + s
                            ins = A(px[:, h % 2, q], bank(name)[:, s * M:(s + 1) * M], ACT.Exp, scale=1 / 16,
                                    bias=nmax[:, h % 2, q:q + 1], accum_out=esum[:, h % 2, q:q + 1])
                        empties(ins, name)

                def xout(h):
                    name = ("xo", l, h, 0)
                    wait_filled(act, name)
                    empties(A(oxT[:, 2 * h], bank(name)[:], ACT.Copy), name)

                xexps(0)
                for h in range(XH):
                    if h + 1 < XH:
                        xexps(h + 1)
                    if h:
                        xout(h - 1)
                    name = ("xp", l, h, 0)
                    wait_filled(act, name)
                    empties(A(pxT[:, h % 2, 0], bank(name)[:], ACT.Copy), name)
                xout(XH - 1)
                norm_squares(NORM_FFN[l])
                norm_out(NORM_FFN[l], f"ln_ffn{l}")
                act.wait_ge(picks_ready, l + 1)
                A(e2[:], e2[:], ACT.Exp).then_inc(gates_exp, 1)

                act.wait_ge(items_ready, l + 1)
                count = act.value_load(item_i[0:1, NX:NX + 1], min_val=0, max_val=NB)
                yd = y_rows[l].rearrange("(a b) c -> a b c", b=BR)
                act.wait_ge(y_zeroed, 32)
                for _ in range(PRE):
                    act.nop().then_inc(y_act[l], 1)
                for b in range(2):
                    act.nop().then_inc(y_stored[l][b], 16)

                def tanh(b, number):
                    act.wait_ge(up_done[l], number + 1 + PRE)
                    A(th[b], ps[2 + b][:, 0:256].rearrange("p (f j) -> p f j", f=FT), ACT.Tanh, scale=0.5
                      ).then_inc(th_done[l], 1)

                def round_w2(b, number, use):
                    act.wait_ge(e_w[l][3 * b + 2], use * 16 + 16)
                    w2 = w2_raw[b]
                    for s in range(2):
                        A(w2_hi[:, 2 * s:2 * s + 2], w2[:, 2 * s:2 * s + 2], ACT.Copy).then_inc(w2_rounded[l], 1)

                round_w2(0, 0, 0)
                tanh(0, 0)
                for i, b, runs in blocks(act, count):
                    with runs(i * 2 + b + 1):
                        tanh(1 - b, i * 2 + b + 1)
                    with runs(i * 2 + b):
                        act.wait_ge(y_stored[l][b], i * 16 + 16)
                        act.wait_ge(down_done[l], i * 2 + b + 1 + PRE)
                        A(y[b][:, 0:HB], ps[4][0:BR, :], ACT.Copy).then_inc(y_act[l], 1)
                        act.wait_ge(y_act[l], i * 2 + b + 1 + PRE)
                        act.wait_ge(y_dve[l], i * 2 + b + 1 + PRE)
                        act.dma_start(yd[bass.ds(i * 2 + b, 1)].rearrange("a b c -> (a b) c"), y[b]
                                      ).then_inc(y_stored[l][b], 16)
                    with runs(i * 2 + b + 1):
                        round_w2(1 - b, i * 2 + b + 1, i + b)
                for b in range(2):
                    act.wait_ge(y_stored[l][b], (count + (1 - b)) // 2 * 16 + 16)
                A(gst[0:1, 0:1], ones[0:1, 0:1], ACT.Copy).then_inc(all_stored, 1)
            norm_squares(6)

        @block.vector
        def _(dve):
            V = nc.vector
            n = [0]

            def link(ins):
                n[0] += 1
                ins.then_inc(dve_chain, 1)
                dve.wait_ge(dve_chain, n[0])

            def norm_scale(norm):
                dve.wait_ge(squares_done, 4 * norm + 4)
                V.tensor_scalar(ss[:], ss[:], 1.0 / C, RMS_EPS, ALU.mult, ALU.add).then_inc(var_ready, 1)
                dve.wait_ge(std_ready, norm + 1)
                link(V.reciprocal(rstd[:], rstd[:]))
                for t in range(TT):
                    V.tensor_scalar(XN[:, t], x[:, t], rstd[:, t:t + 1], None, ALU.mult).then_inc(xn_ready, 1)

            def norm_out(norm, gain):
                for k in range(1, KT, 2):
                    name = ("norm", norm, k)
                    wait_filled(dve, name)
                    empties(V.tensor_scalar(HT[:, k], bank(name)[:], col(gain, k), None, ALU.mult), name)

            def add_out(name, half, t):
                wait_filled(dve, name)
                d = x[:, t, half * HB:(half + 1) * HB]
                empties(V.tensor_tensor(d, bank(name)[:], d, ALU.add), name)

            wait_filled(dve, ("params",))
            nr = len(LN) * KT
            V.tensor_copy(par[:, 0:nr], bank(("params",))[:, 0:nr])
            link(V.tensor_copy(par[:, nr:], bank(("params",))[:, nr:nr + len(RW) * KT]))
            link(V.tensor_scalar(half_w0a0[:], par[:, COL["w0"]:COL["w0"] + 2 * KT], 0.5, None, ALU.mult))
            empties(V.tensor_scalar(one_minus_ka[:], par[:, COL["ka"]:COL["ka"] + KT], -1.0, 1.0, ALU.mult, ALU.add),
                    ("params",))
            norm_scale(0)
            norm_out(0, "ln_mix0")
            wait_filled(dve, ("norm", 0, KT - 1))
            for k in range(0, KT, 2):
                wait_emptied(dve, ("norm", 0, k))
                wait_emptied(dve, ("norm", 0, k + 1))
            dx = tiles(region(1), KT)
            V.tensor_scalar(dx[:, :, 0:1], HT[:, :, 0:1], -1.0, None, ALU.mult)
            link(V.tensor_tensor(dx[:, :, 1:], HT[:, :, :-1], HT[:, :, 1:], ALU.subtract))

            def mix(s, dst):
                for k in range(KT):
                    V.scalar_tensor_tensor(tiles(dst, KT)[:, k], dx[:, k], col(f"mu{s}", k), HT[:, k], ALU.mult,
                                           ALU.add).then_inc(mixed, 1)

            def decays():
                tmp = tiles(g_all, KT)
                for p in range(KT):
                    wait_emptied(dve, ("decay", p))
                    lam = tiles(lam_all, KT)[:, p]
                    link(V.tensor_scalar(tmp[:, p % 4], lam, -0.5 * DECAY, -0.5 * DECAY, ALU.mult, ALU.add))
                    V.tensor_tensor_scan(lam, keep, tmp[:, p % 4], 0.0, ALU.mult, ALU.add).then_inc(scans_done, 1)

            def rates():
                for p in range(KT):
                    wait_emptied(dve, ("rate", p))
                    a = tiles(ak_all, KT)[:, p]
                    V.tensor_scalar(a, a, 0.5, 0.5, ALU.mult, ALU.add)

            dve.wait_ge(ids_zeroed, 32)
            dve.wait_ge(consts, 2)
            mix(1, R[0])
            mix(4, R[1])
            mix(5, R[2])
            wait_emptied(dve, ("hidden_g",))
            V.tensor_scalar(hid_g, hid_g, 0.5, 0.5, ALU.mult, ALU.add).then_inc(hid_g_ready, 1)
            mix(0, R[0])
            mix(2, R[2])
            decays()
            rates()
            wait_filled(dve, ("gate", 1, TT - 1))
            mix(3, RE)

            name = ("knorm",)
            wait_filled(dve, name)
            empties(V.tensor_scalar(krt[:], bank(name)[:, 0:64], 1e-24, None, ALU.max), name)
            wait_emptied(dve, name)
            V.nop().then_inc(kvar_ready, 1)
            dve.wait_ge(kstd_ready, 1)
            V.reciprocal(krt[:], krt[:]).then_inc(krinv_ready, 1)
            name = ("knorm_t",)
            wait_filled(dve, name)
            empties(V.tensor_copy(krT[:], bank(name)[0:NH, :]), name)
            for p in range(KT):
                kraw, kkn, a = (tiles(r, KT)[:, p] for r in (k_all, kk_all, ak_all))
                name = ("kscale", p)
                wait_filled(dve, name)
                ins = V.scalar_tensor_tensor(kkn, kraw, col("kk", p), bank(name)[:], ALU.mult, ALU.mult)
                empties(ins, name)
                tmp = tiles(region(1), KT)[:, p]
                link(V.tensor_scalar(tmp, a, col("ka", p), one_minus_ka[:, p:p + 1], ALU.mult, ALU.add))
                link(V.tensor_tensor(kraw, kraw, tmp, ALU.mult))
                wait_emptied(dve, name)
                V.tensor_tensor(a, kkn, a, ALU.mult)
                V.scalar_tensor_tensor(tmp, tiles(r_all, KT)[:, p], col("rk", p), kraw, ALU.mult, ALU.mult
                                       ).then_inc(prod_ready, 1)
            wait_filled(dve, ("v", 1, TT - 1))
            clear(V, groups[1])
            name = ("bonus",)
            wait_filled(dve, name)
            src = bank(name)[:, 0:64].rearrange("p (t q h) -> p q t h", t=TT, q=PAIRS)
            d = bonus[:].rearrange("p q (t e) -> p q t e", e=2)
            for even in range(2):
                for hh in range(2):
                    last = V.tensor_copy(d[hh * 64:hh * 64 + 64, :, :, even], src[even * 64:even * 64 + 64, :, :, hh])
            empties(last, name)

            dve.wait_ge(pre_done, 2)
            for g in range(2):
                V.nop().then_inc(dve_done[g], 1)
            bs = lambda g, i: ps[4 * g + i][:].rearrange("p (q h t) -> p q h t", q=GP, h=2)
            half_bank = lambda g, i: ps[4 * g + i][:, 0:GP * L].rearrange("p (q t) -> p q t", q=GP)
            with dve.Fori(0, CH) as c:
                for g in range(2):
                    b = groups[g]
                    kk, ak, kc, rc = (chunk_of(r, g, c) for r in (kk_all, ak_all, k_all, r_all))
                    wait_act(dve, g, c, "decay")
                    V.tensor_tensor(b["ar"][:, :, 0, 1:], kk[:, :, 1:], b["dec"][:, :, :-1], ALU.mult).then_inc(dve_done[g], 1)
                    V.tensor_copy(b["ar"][:, :, 0, 0:1], kk[:, :, 0:1]).then_inc(dve_done[g], 1)
                    V.tensor_tensor(b["ar"][:, :, 1, :], rc, b["dec"], ALU.mult).then_inc(dve_done[g], 1)
                    wait_act(dve, g, c, "growth")
                    for src, dst in ((ak, b["beta"]), (kc, b["kappa"])):
                        for h in range(2):
                            r = slice(h * L, (h + 1) * L)
                            V.tensor_tensor(dst[r, :, h, :], src[r], b["gro"][r], ALU.mult).then_inc(dve_done[g], 1)
                for g in range(2):
                    b = groups[g]
                    col_of = lambda i, s: (ps[4 * g + i][:].rearrange("p (q s t) -> p q s t", q=GP, s=2)[:, :, s, :]
                                           .unsqueeze(2).to_broadcast([P, GP, 2, L]))
                    strict, incl, minus_strict, minus_incl = (
                        m.unsqueeze(1).to_broadcast([P, GP, 2, L]) for m in
                        (m_strict[:], m_incl[:], m_minus[:, 0], m_minus[:, 1]))
                    eye = ident[:].rearrange("p (h t) -> p h t", h=2).unsqueeze(1).to_broadcast([P, GP, 2, L])
                    wait_pe(dve, g, c, "gram_b")
                    V.tensor_tensor(b["X"], col_of(0, 0), minus_strict, ALU.mult).then_inc(dve_done[g], 1)
                    wait_dve(dve, g, c, "x0")
                    V.tensor_tensor(b["Tm"], b["X"], eye, ALU.add).then_inc(dve_done[g], 1)
                    V.tensor_tensor(b["Bn"], col_of(0, 1), minus_incl, ALU.mult).then_inc(dve_done[g], 1)
                    wait_pe(dve, g, c, "gram_k")
                    V.tensor_tensor(b["N"], col_of(1, 0), strict, ALU.mult).then_inc(dve_done[g], 1)
                    V.tensor_tensor(b["K"], col_of(1, 1), incl, ALU.mult).then_inc(dve_done[g], 1)
                for i in range(6):
                    for g in range(2):
                        b = groups[g]
                        if i < 4:
                            wait_pe(dve, g, c, f"t{i + 1}" if i else "y1")
                            V.tensor_copy(b["Y"], bs(g, 2)).then_inc(dve_done[g], 1)
                        if i:
                            wait_pe(dve, g, c, f"t{i + 1}")
                            V.tensor_tensor(b["Tm"], bs(g, 3), b["Tm"], ALU.add).then_inc(dve_done[g], 1)
                for g in range(2):
                    b = groups[g]
                    wait_pe(dve, g, c, "s")
                    V.tensor_tensor(b["S"], half_bank(g, 3), b["S"], ALU.add).then_inc(dve_done[g], 1)
                    wait_dve(dve, g, c, "s_add")
                    V.tensor_tensor(b["S"], b["S"], b["dec"][:, :, L - 1:L].to_broadcast([P, GP, L]), ALU.mult
                                    ).then_inc(dve_done[g], 1)

            for g in range(2):
                dve.wait_ge(act_done[g], 1 + CH * len(ACT_S))
                dve.wait_ge(pe_done[g], 1 + CH * len(PE_S))
            n_a = 64 // GS
            o = lambda r, i: sliced(r, i).rearrange("p (a v) -> p a v", v=L)
            of = lambda i: gst[:, i * n_a:(i + 1) * n_a]
            per_row = lambda i: of(i).unsqueeze(2).to_broadcast([P, n_a, L])
            for i in range(GS):
                link(V.tensor_reduce(of(i), o(r_all, i), AX, ALU.add))
                link(V.tensor_scalar(of(i), of(i), 1.0 / L, None, ALU.mult))
                V.tensor_tensor(o(r_all, i), o(r_all, i), per_row(i), ALU.subtract).then_inc(centred, 1)
            dve.wait_ge(centred, GS)
            for i in range(GS):
                dve.wait_ge(gn_sq, i + 1)
                ins = V.tensor_reduce(of(i), o(region(1), i), AX, ALU.add)
            link(ins)
            V.tensor_scalar(gst[:], gst[:], 1.0 / L, GN_EPS, ALU.mult, ALU.add).then_inc(gvar_ready, 1)
            dve.wait_ge(gstd_ready, 1)
            link(V.reciprocal(gst[:], gst[:]))
            dve.wait_ge(gates_done, 4 * CH)
            for i in range(GS):
                link(V.tensor_tensor(o(r_all, i), o(r_all, i), per_row(i), ALU.mult))
                V.tensor_tensor(sliced(r_all, i), sliced(r_all, i), sliced(g_all, i), ALU.mult).then_inc(gn_scaled, 1)
            for p in range(PAIRS):
                for half in range(2):
                    if (2 * p + half) % 2 == 1:
                        unstacks(dve, V.tensor_copy, p, half)
            for half in range(2):
                for t in range(TT):
                    add_out(("rwkv_out", half, t), half, t)

            for l in range(2):
                if l == 1:
                    norm_scale(3)
                    dve.wait_ge(pos_loaded, 16)
                    link(V.tensor_copy(posf[:], posi[:]))
                    a0, a1, a2, a3 = ang
                    g3 = lambda a: a.rearrange("p (t j) -> p t j", t=TT)
                    link(V.tensor_tensor(g3(a0), posf[:].unsqueeze(2).to_broadcast([P, TT, 32]),
                                         inv_freq[:].unsqueeze(1).to_broadcast([P, TT, 32]), ALU.mult))
                    link(V.tensor_scalar(a1, a0, 1 / (2 * math.pi), ROUND_MAGIC, ALU.mult, ALU.add))
                    link(V.tensor_scalar(a1, a1, ROUND_MAGIC, None, ALU.subtract))
                    for part in TWO_PI_PARTS:
                        link(V.scalar_tensor_tensor(a0, a1, -part, a0, ALU.mult, ALU.add))
                    link(V.tensor_scalar(a0, a0, PI_BELOW, -PI_BELOW, ALU.min, ALU.max))
                    link(V.tensor_scalar(a2, a0, -1.0, None, ALU.mult))
                    link(V.tensor_tensor(a2, a2, a0, ALU.max))
                    V.tensor_scalar(a1, a2, -1.0, math.pi / 2, ALU.mult, ALU.add).then_inc(angles_ready, 1)
                    norm_out(3, "ln_mix1")
                    dve.wait_ge(sines_ready, 1)
                    u = 0
                    for stage, dst in (("mq", qm), ("mk", km)):
                        for half in range(2):
                            for t in range(TT):
                                name = (stage, half, t)
                                wait_filled(dve, name)
                                src = bank(name)[:].rearrange("p (h j) -> p h j", j=32)
                                cs = cosn[:, t].unsqueeze(1).to_broadcast([P, 16, 32])
                                sn = sinn[:, t].unsqueeze(1).to_broadcast([P, 16, 32])
                                A_, B_ = (rot[:, u % 4, i].rearrange("p (h j) -> p h j", j=32) for i in range(2))
                                V.tensor_tensor(A_, src, cs, ALU.mult)
                                ins = V.tensor_tensor(B_, src, sn, ALU.mult)
                                empties(ins, name)
                                wait_emptied(dve, name)
                                A4, B4, D4 = (v.rearrange("p (h s) j -> p h s j", s=2) for v in
                                              (A_, B_, dst[:, t, half * HB:(half + 1) * HB]
                                               .rearrange("p (h j) -> p h j", j=32)))
                                V.tensor_tensor(D4[:, :, 0], A4[:, :, 0], B4[:, :, 1], ALU.subtract)
                                V.tensor_tensor(D4[:, :, 1], A4[:, :, 1], B4[:, :, 0], ALU.add).then_inc(rotated, 1)
                                u += 1

                    def maxes(h):
                        for q in range(TT):
                            name = ("ms", h, q)
                            s = bank(name)
                            wait_filled(dve, name)
                            if h >= 2 and q == 0:
                                wait_emptied(dve, ("ms", h - 2, TT - 1))
                            diag = s[:, q * P:(q + 1) * P]
                            link(V.tensor_tensor(diag, diag, m_causal[:], ALU.add))
                            link(V.tensor_reduce(nmax[:, h % 2, q:q + 1], s[:, 0:(q + 1) * P], AX, ALU.max))
                            V.tensor_scalar(nmax[:, h % 2, q:q + 1], nmax[:, h % 2, q:q + 1], -1 / 8, None, ALU.mult
                                            ).then_inc(mmax_ready, 1)

                    def weighted(h):
                        name = ("mo", h)
                        wait_filled(dve, name)
                        src = bank(name)[:, 0:TT * L].rearrange("p (q v) -> p q v", q=TT)
                        empties(V.tensor_tensor(qm[:, :, h * L:(h + 1) * L], src,
                                                einv[:, h % 2, 0:TT].unsqueeze(2).to_broadcast([P, TT, L]), ALU.mult),
                                name)

                    maxes(0)
                    for h in range(NH):
                        if h + 1 < NH:
                            maxes(h + 1)
                        wait_emptied(dve, ("ms", h, TT - 1))
                        for q in range(TT):
                            wait_emptied(dve, ("ms", h, q))
                        if h >= 2:
                            wait_emptied(dve, ("mo", h - 2))
                        link(V.reciprocal(einv[:, h % 2, 0:TT], esum[:, h % 2, 0:TT]))
                        if h:
                            weighted(h - 1)
                    weighted(NH - 1)
                    for k in range(1, KT, 2):
                        wait_filled(dve, ("moT", k))
                        empties(V.tensor_copy(HT[:, k], bank(("moT", k))[:]), ("moT", k))
                    for half in range(2):
                        for t in range(TT):
                            add_out(("moba_out", half, t), half, t)
                dve.wait_ge(mem_loaded, 16 * (l + 1))
                if l == 0:
                    dve.wait_ge(mem_sq, MT)
                    V.tensor_scalar(mss[:], mss[:], 1.0 / C, RMS_EPS, ALU.mult, ALU.add).then_inc(mvar_ready, 1)
                    dve.wait_ge(mstd_ready, 1)
                    link(V.reciprocal(mrstd[:], mrstd[:]))
                for m in range(MT):
                    V.tensor_scalar(memn[:, m], memn[:, m], mrstd[:, m:m + 1], None, ALU.mult).then_inc(memn_ready, 1)
                for i in range(KT // 2):
                    name = ("memT", l, i)
                    wait_filled(dve, name)
                    for s in range(2):
                        k = 2 * i + s
                        ins = V.tensor_scalar(memT[:, k], bank(name)[:, s * M:(s + 1) * M], col(f"ln_kv{l}", k), None,
                                              ALU.mult)
                    empties(ins, name)
                norm_scale(NORM_MEM[l])
                for half in range(2):
                    for m in range(MT):
                        name = ("xv", l, half, m)
                        wait_filled(dve, name)
                        empties(V.tensor_copy(vx[:, m, half * HB:(half + 1) * HB], bank(name)[:]), name)
                norm_out(NORM_MEM[l], f"ln_mem{l}")

                def xmaxes(h):
                    for i in range(2):
                        name = ("xs", l, h, i)
                        wait_filled(dve, name)
                        if h >= 2 and i == 0:
                            dve.wait_ge(xprob_ready, 16 * l + 4 * (h - 2) + 4)
                        nm = nmax[:, h % 2, 2 * i:2 * i + 2]
                        link(V.tensor_reduce(nm, bank(name)[:].rearrange("p (s m) -> p s m", s=2), AX, ALU.max))
                        V.tensor_scalar(nm, nm, -1 / 16, None, ALU.mult).then_inc(xmax_ready, 1)

                def xout(h):
                    name = ("xo", l, h, 1)
                    wait_filled(dve, name)
                    empties(V.tensor_copy(oxT[:, 2 * h + 1], bank(name)[:]), name)

                xmaxes(0)
                for h in range(XH):
                    if h + 1 < XH:
                        xmaxes(h + 1)
                    for i in range(2):
                        wait_emptied(dve, ("xs", l, h, i))
                        link(V.reciprocal(einv[:, h % 2, 2 * i:2 * i + 2], esum[:, h % 2, 2 * i:2 * i + 2]))
                        for q in (2 * i, 2 * i + 1):
                            V.tensor_scalar(px[:, h % 2, q], px[:, h % 2, q], einv[:, h % 2, q:q + 1], None, ALU.mult
                                            ).then_inc(xprob_ready, 1)
                    if h:
                        xout(h - 1)
                    name = ("xp", l, h, 1)
                    wait_filled(dve, name)
                    empties(V.tensor_copy(pxT[:, h % 2, 1], bank(name)[:]), name)
                xout(XH - 1)
                for half in range(2):
                    for t in range(TT):
                        add_out(("xattn_out", l, half, t), half, t)
                norm_scale(NORM_FFN[l])
                norm_out(NORM_FFN[l], f"ln_ffn{l}")

                def bc(a, shape, axis):
                    return a.unsqueeze(axis).to_broadcast(shape)

                def first_of(dst, values, best, width, tmp_):
                    link(V.tensor_tensor(tmp_, values, bc(best, [P, TT, width], 2), ALU.is_lt))
                    link(V.scalar_tensor_tensor(tmp_, tmp_, 1000.0, bc(iota[:, 0:width], [P, TT, width], 1), ALU.mult,
                                                ALU.add))
                    link(V.tensor_reduce(dst, tmp_, AX, ALU.min))

                dve.wait_ge(consts, 2)
                dve.wait_ge(router_loaded, 64 * (l + 1))
                name = ("route", l)
                wait_filled(dve, name)
                ins = V.tensor_tensor(logits, bank(name)[:, 0:TT * 36].rearrange("p (t n) -> p t n", t=TT),
                                      bc(br, [P, TT, 36], 1), ALU.add)
                empties(ins, name)
                wait_emptied(dve, name)
                gl = logits[:, :, 0:G]
                link(V.tensor_reduce(gmax, gl, AX, ALU.max))
                first_of(gidx, gl, gmax, G, t4_)
                link(V.tensor_tensor(g1h, bc(iota[:, 0:G], [P, TT, G], 1), bc(gidx, [P, TT, G], 2), ALU.is_equal))
                link(V.tensor_tensor(prod, logits[:, :, G:].rearrange("p t (g e) -> p t e g", g=G),
                                     bc(g1h, [P, TT, EG, G], 2), ALU.mult))
                link(V.tensor_reduce(sel, prod, AX, ALU.add))
                link(V.tensor_reduce(m1, sel, AX, ALU.max))
                first_of(i1, sel, m1, EG, t8)
                link(V.tensor_tensor(t8, bc(iota[:, 0:EG], [P, TT, EG], 1), bc(i1, [P, TT, EG], 2), ALU.is_equal))
                link(V.scalar_tensor_tensor(sel, t8, NEG, sel, ALU.mult, ALU.add))
                link(V.tensor_reduce(m2, sel, AX, ALU.max))
                first_of(i2, sel, m2, EG, t8)
                link(V.tensor_tensor(e2[:, 0:16].rearrange("p (t g) -> p t g", t=TT), gl, bc(gmax, [P, TT, G], 2),
                                     ALU.subtract))
                V.tensor_tensor(e2[:, 16:20], m2, m1, ALU.subtract).then_inc(picks_ready, 1)
                for o_, i_ in ((o1, i1), (o2, i2)):
                    link(V.scalar_tensor_tensor(i_, gidx, float(EG), i_, ALU.mult, ALU.add))
                    link(V.tensor_tensor(o_, bc(iota, [P, TT, E], 1), bc(i_, [P, TT, E], 2), ALU.is_equal))
                V.tensor_tensor(cnt, o1, o2, ALU.add).then_inc(counts_in, 1)
                dve.wait_ge(gates_exp, l + 1)
                link(V.tensor_reduce(gsum, e2[:, 0:16].rearrange("p (t g) -> p t g", t=TT), AX, ALU.add))
                link(V.scalar_tensor_tensor(gsum, e2[:, 16:20], 1.0, gsum, ALU.add, ALU.mult))
                link(V.reciprocal(gate2[:, 0], gsum))
                link(V.tensor_tensor(gate2[:, 1], gate2[:, 0], e2[:, 16:20], ALU.mult))
                link(V.memset(one32, 1.0))
                link(V.tensor_scalar(step7, iota[:, 0:7], float(BR), float(BR), ALU.mult, ALU.add))
                name = ("rank", l)
                wait_filled(dve, name)
                rk_ps = bank(name)[:, 0:5 * E].rearrange("p (t e) -> p t e", e=E)
                link(V.scalar_tensor_tensor(rank, bc(iota, [P, TT, E], 1), float(BR), rk_ps[:, 0:TT], ALU.mult, ALU.add))
                link(V.tensor_scalar(extra, rk_ps[:, 0:TT], float(BR), None, ALU.is_ge))
                ins = V.tensor_tensor(t32, bc(rk_ps[:, TT], [P, E, 7], 2), bc(step7, [P, E, 7], 1), ALU.is_gt)
                empties(ins, name)
                wait_emptied(dve, name)
                link(V.tensor_reduce(nblk, t32, AX, ALU.add))
                link(V.tensor_tensor_scan(cum, one32, nblk, 0.0, ALU.mult, ALU.add))
                link(V.tensor_tensor(nblk, cum, nblk, ALU.subtract))
                link(V.scalar_tensor_tensor(nblk, nblk, float(E - 1), iota, ALU.add, ALU.subtract))
                link(V.tensor_tensor(extra, extra, bc(nblk, [P, TT, E], 1), ALU.mult))
                link(V.scalar_tensor_tensor(rank, extra, float(BR), rank, ALU.mult, ALU.add))
                for k, o_ in enumerate((o1, o2)):
                    link(V.tensor_tensor(o_, o_, rank, ALU.mult))
                    link(V.tensor_reduce(dst2[:, k], o_, AX, ALU.add))
                V.tensor_copy(dest_i[:], dst2).then_inc(dest_ready, 1)
                link(V.tensor_tensor(itemc[0:1], bc(cum[0:1], [1, NX, E], 1), bc(item_no[:], [1, NX, E], 2),
                                     ALU.is_le))
                link(V.tensor_reduce(itf[0:1, 0:NX], itemc[0:1], AX, ALU.add))
                link(V.tensor_scalar(itf[0:1, 0:NX], itf[0:1, 0:NX], float(E - 1), None, ALU.min))
                link(V.tensor_scalar(itf[0:1, NX:NX + 1], cum[0:1, E - 1:E], float(E), None, ALU.add))
                V.tensor_copy(item_i[:], itf[0:1]).then_inc(items_ready, 1)

                dve.wait_ge(items_ready, l + 1)
                count = dve.value_load(item_i[0:1, NX:NX + 1], min_val=0, max_val=NB)
                gain = par[:, COL[f"ln_ffn{l}"]:COL[f"ln_ffn{l}"] + KT].unsqueeze(2).to_broadcast([P, KT, BR])

                def rows_out(b, number):
                    dve.wait_ge(rowsT[l], number + PRE)
                    V.tensor_tensor(hgT[b], ps[b][:].rearrange("p (k j) -> p k j", k=KT), gain, ALU.mult
                                    ).then_inc(rowsT_out[l], 1)

                for _ in range(PRE):
                    dve.nop().then_inc(y_dve[l], 1)
                    dve.nop().then_inc(act_ready[l], 1)

                def gated(b, number):
                    dve.wait_ge(th_done[l], number + 1)
                    u1 = ps[2 + b][:, 0:256].rearrange("p (f j) -> p f j", f=FT)
                    u3 = ps[2 + b][:, 256:512].rearrange("p (f j) -> p f j", f=FT)
                    V.scalar_tensor_tensor(ga[b], th[b], 1.0, u1, ALU.add, ALU.mult).then_inc(a_part[l], 1)
                    dve.wait_ge(a_part[l], number * 3 + 1)
                    V.scalar_tensor_tensor(hact[b], ga[b], 0.5, u3, ALU.mult, ALU.mult).then_inc(a_part[l], 1)
                    dve.wait_ge(a_part[l], number * 3 + 2)
                    V.tensor_copy(h_hi[b][:], hact[b]).then_inc(a_part[l], 1)
                    dve.wait_ge(a_part[l], number * 3 + 3)
                    V.tensor_tensor(h_lo[b][:], hact[b], h_hi[b][:].bitcast(F32), ALU.subtract
                                    ).then_inc(act_ready[l], 1)

                def rest_w2(b, number):
                    w2 = w2_raw[b]
                    for s in range(2):
                        dve.wait_ge(w2_rounded[l], number * 2 + s + 1)
                        V.tensor_tensor(w2_lo[:, 2 * s:2 * s + 2], w2[:, 2 * s:2 * s + 2],
                                        w2_hi[:, 2 * s:2 * s + 2].bitcast(F32), ALU.subtract).then_inc(w2_split[l], 1)

                rows_out(0, 1)
                rest_w2(0, 0)
                rows_out(1, 2)
                gated(0, 0)
                for i, b, runs in blocks(dve, count):
                    with runs(i * 2 + b + 1):
                        gated(1 - b, i * 2 + b + 1)
                        rows_out(b, i * 2 + b + 3)
                    with runs(i * 2 + b):
                        dve.wait_ge(y_stored[l][b], i * 16 + 16)
                        dve.wait_ge(down_done[l], i * 2 + b + 1 + PRE)
                        V.tensor_copy(y[b][:, HB:2 * HB], ps[5][0:BR, :]).then_inc(y_dve[l], 1)
                    with runs(i * 2 + b + 1):
                        rest_w2(1 - b, i * 2 + b + 1)
                for s in range(8):
                    t, k = s // 2, s % 2
                    dve.wait_ge(combined_loaded[l][s], 16)
                    V.scalar_tensor_tensor(x[:, t], combined[s], gate2[:, k, t:t + 1], x[:, t], ALU.mult, ALU.add
                                           ).then_inc(x_updated, 1)
                    dve.wait_ge(x_updated, 8 * l + s + 1)
            norm_scale(6)
            dve.wait_ge(lnf_loaded, 16)
            dve.wait_ge(xn_ready, 28)
            for t in range(TT):
                V.tensor_tensor(XN[:, t], XN[:, t], R[2][:, 0:C], ALU.mult).then_inc(out_ready, 1)

        @block.tensor
        def _(pe):
            nxt = [0]
            mm = nc.tensor.matmul

            def start(name):
                assert ORDER[nxt[0]] == name, (ORDER[nxt[0]], name)
                g = nxt[0]
                nxt[0] += 1
                if g >= 8:
                    pe.wait_ge(emptied[g % 8], g // 8)
                return ps[g % 8]

            def finish(ins):
                ins.then_inc(filled, 1)

            def weights(stage, half):
                j = load_index(stage, half)
                pe.wait_ge(w_loaded[j % 2], 16 * (j // 2 + 1))
                return W[j % 2]

            def transpose_norm(norm):
                for k in range(KT):
                    d = start(("norm", norm, k))
                    for t in range(TT):
                        if k == 0:
                            pe.wait_ge(xn_ready, 4 * norm + t + 1)
                        ins = nc.tensor.transpose(d[:, t * P:(t + 1) * P], XN[:, t, k * P:(k + 1) * P], ident[:])
                    finish(ins)

            def ht_ready(norm, k):
                wait_emptied(pe, ("norm", norm, k))

            def to_channels(stage, rhs, ready, n=T):
                for j in range(KT):
                    w = weights(stage, j // 4) if j % 4 == 0 else w
                    d = start(stage + (j,))
                    for k in range(KT):
                        if j == 0:
                            ready(k)
                        ins = mm(d[:, 0:n], lhsT=w[:, k, (j % 4) * P:(j % 4 + 1) * P], rhs=rhs[:, k, 0:n],
                                 start=k == 0, stop=k == KT - 1)
                    finish(ins)

            def to_tokens(stage, lhs, ready, nt=TT):
                for half in range(2):
                    w = weights(stage, half)
                    for t in range(nt):
                        d = start(stage + (half, t))
                        for k in range(KT):
                            if half == 0 and t == 0:
                                ready(k)
                            ins = mm(d[:], lhsT=lhs[:, k, t * P:(t + 1) * P], rhs=w[:, k, :], start=k == 0,
                                     stop=k == KT - 1)
                        finish(ins)

            pe.wait_ge(consts, 1)
            pe.wait_ge(params_loaded, 16 * 10)
            d = start(("params",))
            nc.tensor.transpose(d[:, 0:64], prow[0:64, :], ident[0:64, 0:64])
            finish(nc.tensor.transpose(d[:, 64:152], qrow[0:88, :], ident[0:88, 0:88]))
            transpose_norm(0)

            mix_ready = lambda s: (lambda k: pe.wait_ge(mixed, s * KT + k + 1))
            xs = [tiles(R[i], KT) for i in range(3)]
            d = start(("hidden_wa",))
            pe.wait_ge(lora_loaded, 16 * 6)
            for k in range(KT):
                mix_ready(0)(k)
                mm(d[0:64, :], lhsT=lw1[:, k], rhs=xs[0][:, k], start=k == 0, stop=k == KT - 1)
            for k in range(KT):
                mix_ready(1)(k)
                ins = mm(d[64:128, :], lhsT=la1[:, k], rhs=xs[1][:, k], start=k == 0, stop=k == KT - 1)
            finish(ins)
            d = start(("hidden_g",))
            for k in range(KT):
                mix_ready(2)(k)
                ins = mm(d[:], lhsT=lg1[:, k], rhs=xs[2][:, k], start=k == 0, stop=k == KT - 1)
            finish(ins)
            wait_emptied(pe, ("hidden_wa",))
            for p in range(KT):
                finish(mm(start(("decay", p))[:], lhsT=lwa2[0:64, p * P:(p + 1) * P], rhs=hid_wa[0:64, :], start=True,
                          stop=True))
            for p in range(KT):
                finish(mm(start(("rate", p))[:], lhsT=lwa2[64:128, p * P:(p + 1) * P], rhs=hid_wa[64:128, :],
                          start=True, stop=True))
            pe.wait_ge(hid_g_ready, 1)
            for half in range(2):
                for t in range(TT):
                    finish(mm(start(("gate", half, t))[:], lhsT=hid_g[:, t * P:(t + 1) * P],
                              rhs=lg2[:, half * HB:(half + 1) * HB], start=True, stop=True))
            to_channels(("r",), xs[0], mix_ready(3))
            to_channels(("k",), xs[2], mix_ready(4))
            def v_tile(half, t):
                w = weights(("v",), half)
                d = start(("v", half, t))
                for k in range(KT):
                    mix_ready(5)(k)
                    ins = mm(d[:], lhsT=tiles(RE, KT)[:, k, t * P:(t + 1) * P], rhs=w[:, k, :], start=k == 0,
                             stop=k == KT - 1)
                finish(ins)

            for t in range(TT):
                v_tile(0, t)
            pe.wait_ge(consts, 2)
            d = start(("knorm",))
            for t in range(TT):
                for p in range(KT):
                    pe.wait_ge(kk_sq, p + 1)
                    c0 = (t * KT + p) * 2
                    ins = mm(d[:, c0:c0 + 2], lhsT=tiles(region(1), KT)[:, p, t * P:(t + 1) * P], rhs=pair_sel[:],
                             start=True, stop=True)
            finish(ins)
            v_tile(1, 0)
            pe.wait_ge(krinv_ready, 1)
            d = start(("knorm_t",))
            for t in range(TT):
                ins = nc.tensor.transpose(d[0:NH, t * P:(t + 1) * P], krt[:, t * NH:(t + 1) * NH], ident[:])
            finish(ins)
            wait_emptied(pe, ("knorm_t",))
            for t, scaled in enumerate(KSCALES):
                if t:
                    v_tile(1, t)
                for p in scaled:
                    finish(mm(start(("kscale", p))[:], lhsT=head_sel[:, p, :], rhs=krT[:], start=True, stop=True))
            d = start(("bonus",))
            for t in range(TT):
                for p in range(KT):
                    pe.wait_ge(prod_ready, p + 1)
                    c0 = (t * KT + p) * 2
                    ins = mm(d[:, c0:c0 + 2], lhsT=tiles(region(1), KT)[:, p, t * P:(t + 1) * P], rhs=pair_sel[:],
                             start=True, stop=True)
            finish(ins)

            for name in ORDER[nxt[0] - 8:nxt[0]]:
                wait_emptied(pe, name)
            pe.wait_ge(pre_done, 2)
            for g in range(2):
                pe.nop().then_inc(pe_done[g], 1)
            def each_pair(dst, width, *terms):
                for q in range(GP):
                    for i, (lhs, rhs) in enumerate(terms):
                        ins = mm(dst[:, q * width:(q + 1) * width], lhsT=lhs(q), rhs=rhs(q), start=i == 0,
                                 stop=i == len(terms) - 1)
                return ins

            square = lambda m: (lambda q: m[:, q].rearrange("p h t -> p (h t)"))
            thin = lambda m: (lambda q: m[:, q])
            with pe.Fori(0, CH) as c:
                for g in range(2):
                    b, bank4 = groups[g], ps[4 * g:4 * g + 4]
                    wait_dve(pe, g, c, "kappa1")
                    ar = lambda q: b["ar"][:, q].rearrange("p s t -> p (s t)")
                    each_pair(bank4[0], P, (square(b["beta"]), ar)).then_inc(pe_done[g], 1)
                    each_pair(bank4[1], P, (square(b["kappa"]), ar)).then_inc(pe_done[g], 1)
                    for i, m in ((2, b["beta"]), (3, b["kappa"])):
                        for q in range(GP):
                            ins = nc.tensor.transpose(bank4[i][:, q * P:(q + 1) * P], square(m)(q), ident[:])
                        ins.then_inc(pe_done[g], 1)
                for g in range(2):
                    b, bank4 = groups[g], ps[4 * g:4 * g + 4]
                    wait_dve(pe, g, c, "bn")
                    for q in range(GP):
                        ins = nc.tensor.transpose(bank4[0][:, q * P:(q + 1) * P], square(b["X"])(q), ident[:])
                    ins.then_inc(pe_done[g], 1)
                for i in range(6):
                    for g in range(2):
                        b, bank4 = groups[g], ps[4 * g:4 * g + 4]
                        X, Y, Tm = square(b["X"]), square(b["Y"]), square(b["Tm"])
                        if i == 0:
                            wait_act(pe, g, c, "y0")
                            wait_dve(pe, g, c, "k")
                        else:
                            wait_act(pe, g, c, f"x{i}" if i < 5 else "y5")
                            if i < 5:
                                wait_dve(pe, g, c, f"t{i}" if i > 1 else "y1")
                            else:
                                wait_dve(pe, g, c, "t5")
                        if i < 4:
                            each_pair(bank4[1], P, (Y, X)).then_inc(pe_done[g], 1)
                        if i < 5:
                            each_pair(bank4[2], P, (X, Y)).then_inc(pe_done[g], 1)
                        if i:
                            each_pair(bank4[3], P, (Y, Tm)).then_inc(pe_done[g], 1)
                v = lambda g: (lambda q: chunk_of(v_all, g, c)[:, q])
                for g in range(2):
                    b, bank4 = groups[g], ps[4 * g:4 * g + 4]
                    wait_act(pe, g, c, "rho1")
                    each_pair(bank4[0], L, (square(b["N"]), v(g)), (square(b["alpha"]), thin(b["S"]))).then_inc(pe_done[g], 1)
                for g in range(2):
                    b, bank4 = groups[g], ps[4 * g:4 * g + 4]
                    wait_act(pe, g, c, "rhs")
                    wait_dve(pe, g, c, "t6")
                    each_pair(bank4[1], L, (square(b["Tm"]), thin(b["rhs"]))).then_inc(pe_done[g], 1)
                for g in range(2):
                    b, bank4 = groups[g], ps[4 * g:4 * g + 4]
                    wait_act(pe, g, c, "u")
                    each_pair(bank4[2], L, (square(b["rho"]), thin(b["S"])), (square(b["Bn"]), thin(b["u"])),
                              (square(b["K"]), v(g))).then_inc(pe_done[g], 1)
                    each_pair(bank4[3], L, (square(b["bt"]), thin(b["u"])), (square(b["kt"]), v(g))).then_inc(pe_done[g], 1)

            for p in range(PAIRS):
                pe.wait_ge(gn_done, p * GS // PAIRS + 1)
                for half in range(2):
                    d = start(("gn_t", p, half))
                    for c in range(4):
                        ins = nc.tensor.transpose(d[0:64, c * P:(c + 1) * P], by_chunk(r_all)[:, p, half * 4 + c, :],
                                                  ident[:])
                    finish(ins)

            def gn_ready(k):
                wait_emptied(pe, ("gn_t", k, 0))
                wait_emptied(pe, ("gn_t", k, 1))

            to_tokens(("rwkv_out",), HT, gn_ready)

            for l in range(2):
                if l == 1:
                    transpose_norm(3)
                    for i, s in enumerate(("mq", "mk", "mv")):
                        to_tokens((s,), HT, (lambda k: ht_ready(3, k)) if i == 0 else (lambda k: None))
                    for stage, src, base in (("mqT", qm, 0), ("mkT", km, 8)):
                        for p in range(KT):
                            d = start((stage, p))
                            for t in range(TT):
                                pe.wait_ge(rotated, base + (p // 4) * TT + t + 1)
                                ins = nc.tensor.transpose(d[:, t * P:(t + 1) * P], src[:, t, p * P:(p + 1) * P],
                                                          ident[:])
                            finish(ins)

                    def scores(h):
                        p, r = h // 2, slice((h % 2) * L, (h % 2 + 1) * L)
                        for q in range(TT):
                            d = start(("ms", h, q))
                            if h % 2 == 0 and q == 0:
                                wait_emptied(pe, ("mqT", p))
                                wait_emptied(pe, ("mkT", p))
                            w = (q + 1) * P
                            finish(mm(d[:, 0:w], lhsT=qmT[r, p, q * P:(q + 1) * P], rhs=kmT[r, p, 0:w], start=True,
                                      stop=True))

                    def values(h):
                        d = start(("mo", h))
                        for q in range(TT):
                            wait_emptied(pe, ("mp", h, q))
                            for j in range(q + 1):
                                ins = mm(d[:, q * L:(q + 1) * L], lhsT=pmT[:, h % 2, q, j * P:(j + 1) * P],
                                         rhs=vm[:, j, h * L:(h + 1) * L], start=j == 0, stop=j == q)
                        finish(ins)

                    for t in range(2 * TT):
                        wait_emptied(pe, ("mv", t // TT, t % TT))
                    scores(0)
                    for h in range(NH):
                        if h + 1 < NH:
                            scores(h + 1)
                        for q in range(TT):
                            d = start(("mp", h, q))
                            wait_emptied(pe, ("ms", h, q))
                            for j in range(q + 1):
                                ins = nc.tensor.transpose(d[:, j * P:(j + 1) * P], pm[:, h % 2, q, j * P:(j + 1) * P],
                                                          ident[:])
                            finish(ins)
                        if h:
                            values(h - 1)
                    values(NH - 1)
                    for k in range(KT):
                        d = start(("moT", k))
                        wait_emptied(pe, ("mo", 2 * k + 1))
                        wait_emptied(pe, ("mo", 2 * k))
                        for t in range(TT):
                            ins = nc.tensor.transpose(d[:, t * P:(t + 1) * P], qm[:, t, k * P:(k + 1) * P], ident[:])
                        finish(ins)
                    to_tokens(("moba_out",), HT, lambda k: wait_emptied(pe, ("moT", k)))

                for i in range(KT // 2):
                    d = start(("memT", l, i))
                    for s in range(2):
                        for m in range(MT):
                            pe.wait_ge(memn_ready, MT * l + m + 1)
                            k = 2 * i + s
                            ins = nc.tensor.transpose(d[:, s * M + m * P:s * M + (m + 1) * P],
                                                      memn[:, m, k * P:(k + 1) * P], ident[:])
                    finish(ins)
                to_channels(("xk", l), memT, lambda k: wait_emptied(pe, ("memT", l, k // 2)), n=M)
                to_tokens(("xv", l), memT, lambda k: None, nt=MT)
                transpose_norm(NORM_MEM[l])
                to_channels(("xq", l), HT, lambda k: ht_ready(NORM_MEM[l], k))

                def xscores(h):
                    for i in range(2):
                        d = start(("xs", l, h, i))
                        if i == 0:
                            for c in (2 * h, 2 * h + 1):
                                wait_emptied(pe, ("xq", l, c))
                                wait_emptied(pe, ("xk", l, c))
                        for s in range(2):
                            q = 2 * i + s
                            for c in range(2):
                                ins = mm(d[:, s * M:(s + 1) * M], lhsT=qxT[:, 2 * h + c, q * P:(q + 1) * P],
                                         rhs=kxT[:, 2 * h + c, :], start=c == 0, stop=c == 1)
                        finish(ins)

                def xvalues(h):
                    for c in range(2):
                        d = start(("xo", l, h, c))
                        for m in range(MT):
                            if h == 0 and c == 0:
                                wait_emptied(pe, ("xv", l, 0, m))
                                wait_emptied(pe, ("xv", l, 1, m))
                            wait_emptied(pe, ("xp", l, h, m))
                            ins = mm(d[:], lhsT=vx[:, m, h * XD + c * P:h * XD + (c + 1) * P], rhs=pxT[:, h % 2, m],
                                     start=m == 0, stop=m == MT - 1)
                        finish(ins)

                xscores(0)
                for h in range(XH):
                    if h + 1 < XH:
                        xscores(h + 1)
                    if h:
                        xvalues(h - 1)
                    for m in range(MT):
                        d = start(("xp", l, h, m))
                        for q in range(TT):
                            pe.wait_ge(xprob_ready, 16 * l + 4 * h + q + 1)
                            ins = nc.tensor.transpose(d[:, q * P:(q + 1) * P], px[:, h % 2, q, m * P:(m + 1) * P],
                                                      ident[:])
                        finish(ins)
                xvalues(XH - 1)
                to_tokens(("xattn_out", l), oxT, lambda k: wait_emptied(pe, ("xo", l, k // 2, k % 2)))

                transpose_norm(NORM_FFN[l])
                pe.wait_ge(router_loaded, 64 * (l + 1))
                d = start(("route", l))
                for t in range(TT):
                    for k in range(KT):
                        if t == 0:
                            ht_ready(NORM_FFN[l], k)
                        ins = mm(d[:, t * 36:(t + 1) * 36], lhsT=HT[:, k, t * P:(t + 1) * P], rhs=wr[:, k, :],
                                 start=k == 0, stop=k == KT - 1)
                finish(ins)
                pe.wait_ge(counts_in, l + 1)
                pe.wait_ge(consts, 2)
                d = start(("rank", l))
                for t in range(TT + 1):
                    for j in range(min(t + 1, TT)):
                        last = j == min(t, TT - 1)
                        ins = mm(d[:, t * E:(t + 1) * E], lhsT=before[:] if j == t else ones[:], rhs=cnt[:, j],
                                 start=j == 0, stop=last)
                finish(ins)

                wait_emptied(pe, ("rank", l))
                for name in ORDER[nxt[0] - 8:nxt[0]]:
                    wait_emptied(pe, name)
                pe.wait_ge(items_ready, l + 1)
                count = pe.value_load(item_i[0:1, NX:NX + 1], min_val=0, max_val=NB)

                def rows_in(b):
                    for k in range(KT):
                        ins = nc.tensor.transpose(ps[b][:, k * BR:(k + 1) * BR], hg[b][:, k * P:(k + 1) * P],
                                                  ident[0:BR, 0:BR])
                    ins.then_inc(rowsT[l], 1)

                for _ in range(PRE):
                    pe.nop().then_inc(up_done[l], 1)
                    pe.nop().then_inc(down_done[l], 1)
                    pe.nop().then_inc(rowsT[l], 1)

                def up(b, number, use, next_use):
                    pe.wait_ge(rowsT_out[l], number + 1)
                    pe.wait_ge(act_ready[l], number - 1 + PRE)
                    for s in range(2):
                        w = ew[b][s].rearrange("p (k n) -> p k n", k=KT)
                        pe.wait_ge(e_w[l][3 * b + s], use * 16 + 16)
                        if s == 1:
                            pe.wait_ge(gathered[l][1 - b], next_use * 16 + 16)
                        for f in range(FT):
                            c0 = s * 256 + f * BR
                            for k in range(KT):
                                ins = mm(ps[2 + b][:, c0:c0 + BR], lhsT=w[:, k, f * P:(f + 1) * P],
                                         rhs=hgT[b][:, k], start=k == 0, stop=k == KT - 1)
                    ins.then_inc(up_done[l], 1)
                    rows_in(1 - b)

                def keep_clock(n):
                    for _ in range(n):
                        mm(ps[6][:, 0:256], lhsT=zero[:, 0:P], rhs=zero[:], start=True, stop=True)

                pe.wait_ge(ids_stored, 16 * 8 * (l + 1))
                keep_clock(10)
                pe.wait_ge(gathered[l][0], 16)
                keep_clock(4)
                rows_in(0)
                keep_clock(3)
                up(0, 0, 0, 0)
                keep_clock(3)
                for i, b, runs in blocks(pe, count):
                    with runs(i * 2 + b + 1):
                        up(1 - b, i * 2 + b + 1, i + b, i + 1)
                    with runs(i * 2 + b):
                        pe.wait_ge(act_ready[l], i * 2 + b + 1 + PRE)
                        pe.wait_ge(w2_split[l], (i * 2 + b) * 2 + 2)
                        pe.wait_ge(y_act[l], i * 2 + b + PRE)
                        pe.wait_ge(y_dve[l], i * 2 + b + PRE)
                        for half in range(2):
                            for f in range(FT):
                                n = slice(half * HB, (half + 1) * HB)
                                for i_, (h_, w_) in enumerate(((h_hi, w2_hi), (h_lo, w2_hi), (h_hi, w2_lo))):
                                    ins = mm(ps[4 + half][0:BR, :], lhsT=h_[b][:, f], rhs=w_[:, f, n],
                                             start=f == 0 and i_ == 0, stop=f == FT - 1 and i_ == 2)
                        ins.then_inc(down_done[l], 1)


_INS = ["x", "mem", "positions", "ln_mix", "ln_mem", "ln_memkv", "ln_ffn", "rw_mu", "rw_w0", "rw_w1", "rw_w2", "rw_a0",
        "rw_a1", "rw_a2", "rw_g1", "rw_g2", "rw_kk", "rw_ka", "rw_rk", "rw_wrkv", "rw_lnx_g", "rw_lnx_b", "rw_wo",
        "mb_wqkv", "mb_wo", "mx_wq", "mx_wkv", "mx_wo", "moe_wg", "moe_bg", "moe_we", "moe_be", "moe_w1", "moe_w3",
        "moe_w2", "ln_f"]


def kernel(**inputs):
    import numpy as _np
    import concourse.bacc as _bacc
    from concourse import mybir as _mybir
    from concourse.bass_utils import run_bass_kernel_spmd as _run

    nc = _bacc.Bacc("TRN2", target_bir_lowering=False, num_devices=1)
    arrays, args = {}, []
    for name in _INS:
        a = _np.ascontiguousarray(inputs[name])
        arrays[f"in_{name}"] = a
        args.append(nc.dram_tensor(f"in_{name}", a.shape, _mybir.dt.from_np(a.dtype), kind="ExternalInput").ap())
    args.append(nc.dram_tensor("out_0", (1, 512, 1024), _mybir.dt.float32, kind="ExternalOutput").ap())
    trunk(nc, *args)
    r = _run(nc, [arrays], core_ids=[0])
    return r.results[0]["out_0"]
```
